# Optimizing a Trainium2 kernel written in Bass

```python
import math
import jax
import jax.numpy as jnp
from jax import lax
import numpy as np
import jax, jax.numpy as jnp

D_MODEL = 1024
BATCH = 1
SEQ = 256
DEPTH = 1

HEAD_DIM = 64
BRANCH_WIDTH = D_MODEL // 2
N_BRANCH = 3
CONV_WIDTH = BRANCH_WIDTH
CONV_K = 3
FOX_HEADS = BRANCH_WIDTH // HEAD_DIM
SWA_HEADS = BRANCH_WIDTH // HEAD_DIM
SWA_KV_HEADS = 2
SWA_GROUP = SWA_HEADS // SWA_KV_HEADS
WINDOW = 128
BLOCK = 128
N_BUCKETS = 32
MAX_DISTANCE = WINDOW
MEM_LEN = 256
X_HEADS = 4
X_HEAD_DIM = D_MODEL // X_HEADS
_FF_RAW = -(-8 * D_MODEL // 3)
D_FF = -(-_FF_RAW // 256) * 256
IN_COLS = (3 * CONV_WIDTH + 3 * FOX_HEADS * HEAD_DIM + FOX_HEADS
           + (SWA_HEADS + 2 * SWA_KV_HEADS) * HEAD_DIM + N_BRANCH * D_MODEL)
RMS_EPS = 1e-6
NEG_INF = -1e30


def rms_norm(x, g):
    xf = x.astype(jnp.float32)
    y = xf * lax.rsqrt(jnp.mean(xf * xf, axis=-1, keepdims=True) + RMS_EPS)
    return (y * g.astype(jnp.float32)).astype(x.dtype)

def split_proj(proj):
    sizes = ([CONV_WIDTH] * 3 + [FOX_HEADS * HEAD_DIM] * 3 + [FOX_HEADS]
             + [SWA_HEADS * HEAD_DIM, SWA_KV_HEADS * HEAD_DIM, SWA_KV_HEADS * HEAD_DIM]
             + [N_BRANCH * D_MODEL])
    parts, off = [], 0
    for s in sizes:
        parts.append(proj[..., off:off + s])
        off += s
    return parts

def short_conv_branch(gate_b, gate_c, u, conv_w):
    z = gate_c * u
    y = lax.conv_general_dilated(
        z, conv_w[:, None, :].astype(z.dtype), window_strides=(1,),
        padding=[(CONV_K - 1, 0)], dimension_numbers=('NWC', 'WIO', 'NWC'),
        feature_group_count=CONV_WIDTH)
    return gate_b * y

def fox_branch(q, k, v, f_logit, f_bias):
    b, s = q.shape[0], q.shape[1]
    nb = s // BLOCK
    q = q.reshape(b, s, FOX_HEADS, HEAD_DIM)
    k = k.reshape(b, s, FOX_HEADS, HEAD_DIM)
    v = v.reshape(b, s, FOX_HEADS, HEAD_DIM)
    log_f = jax.nn.log_sigmoid(f_logit.astype(jnp.float32) + f_bias.astype(jnp.float32))
    c = jnp.cumsum(log_f, axis=1)
    c_k = c.transpose(0, 2, 1)
    q_blocks = q.reshape(b, nb, BLOCK, FOX_HEADS, HEAD_DIM).transpose(1, 0, 2, 3, 4)
    c_blocks = c.reshape(b, nb, BLOCK, FOX_HEADS).transpose(1, 0, 2, 3)
    starts = jnp.arange(nb, dtype=jnp.int32) * BLOCK
    k_pos = jnp.arange(s, dtype=jnp.int32)
    scale = HEAD_DIM ** -0.5

    def one_block(args):
        qi, ci, start = args
        logits = jnp.einsum('bqhd,bkhd->bhqk', qi, k).astype(jnp.float32) * scale
        logits = logits + ci.transpose(0, 2, 1)[..., None] - c_k[:, :, None, :]
        q_pos = start + jnp.arange(BLOCK, dtype=jnp.int32)
        causal = k_pos[None, :] <= q_pos[:, None]
        logits = jnp.where(causal[None, None], logits, NEG_INF)
        p = jax.nn.softmax(logits, axis=-1)
        return jnp.einsum('bhqk,bkhd->bqhd', p.astype(v.dtype), v)

    out = lax.map(one_block, (q_blocks, c_blocks, starts))
    return out.transpose(1, 0, 2, 3, 4).reshape(b, s, FOX_HEADS * HEAD_DIM)

def t5_bucket(n):
    n = jnp.maximum(n, 0)
    max_exact = N_BUCKETS // 2
    large = max_exact + (
        jnp.log(jnp.maximum(n, 1).astype(jnp.float32) / max_exact)
        / math.log(MAX_DISTANCE / max_exact) * (N_BUCKETS - max_exact)).astype(jnp.int32)
    large = jnp.minimum(large, N_BUCKETS - 1)
    return jnp.where(n < max_exact, n, large)

def swa_sink_branch(q, k, v, rel_bias, sink):
    b, s = q.shape[0], q.shape[1]
    nb = s // BLOCK
    qb = q.reshape(b, nb, BLOCK, SWA_KV_HEADS, SWA_GROUP, HEAD_DIM)
    kb = k.reshape(b, nb, BLOCK, SWA_KV_HEADS, HEAD_DIM)
    vb = v.reshape(b, nb, BLOCK, SWA_KV_HEADS, HEAD_DIM)

    def band(t):
        prev = jnp.concatenate([jnp.zeros_like(t[:, :1]), t[:, :-1]], axis=1)
        return jnp.concatenate([prev, t], axis=2)

    k_band, v_band = band(kb), band(vb)
    tq = jnp.arange(BLOCK, dtype=jnp.int32)
    sk = jnp.arange(2 * BLOCK, dtype=jnp.int32)
    dist = BLOCK + tq[:, None] - sk[None, :]
    in_window = (dist >= 0) & (dist < WINDOW)
    key_pos = jnp.arange(nb, dtype=jnp.int32)[:, None] * BLOCK - BLOCK + sk[None, :]
    mask = in_window[None] & (key_pos >= 0)[:, None, :]
    bias = rel_bias.astype(jnp.float32)[t5_bucket(dist)]
    bias = bias.reshape(BLOCK, 2 * BLOCK, SWA_KV_HEADS, SWA_GROUP).transpose(2, 3, 0, 1)
    logits = jnp.einsum('bnqkgd,bnskd->bnkgqs', qb, k_band).astype(jnp.float32) * HEAD_DIM ** -0.5
    logits = jnp.where(mask[None, :, None, None], logits + bias, NEG_INF)
    sink_l = sink.astype(jnp.float32).reshape(SWA_KV_HEADS, SWA_GROUP)[None, None, :, :, None]
    m = jnp.maximum(logits.max(axis=-1), sink_l)
    p = jnp.exp(logits - m[..., None])
    denom = p.sum(axis=-1) + jnp.exp(sink_l - m)
    p = p / denom[..., None]
    out = jnp.einsum('bnkgqs,bnskd->bnqkgd', p.astype(v.dtype), v_band)
    return out.reshape(b, s, SWA_HEADS * HEAD_DIM)

def cross_attention(xn, mem_n, w_q, w_kv, w_o):
    b, s = xn.shape[0], xn.shape[1]
    q = (xn @ w_q).reshape(b, s, X_HEADS, X_HEAD_DIM)
    kv = mem_n @ w_kv
    k = kv[..., :X_HEADS * X_HEAD_DIM].reshape(b, -1, X_HEADS, X_HEAD_DIM)
    v = kv[..., X_HEADS * X_HEAD_DIM:].reshape(b, -1, X_HEADS, X_HEAD_DIM)
    logits = jnp.einsum('bshd,bmhd->bhsm', q, k).astype(jnp.float32) * X_HEAD_DIM ** -0.5
    p = jax.nn.softmax(logits, axis=-1)
    o = jnp.einsum('bhsm,bmhd->bshd', p.astype(v.dtype), v).reshape(b, s, X_HEADS * X_HEAD_DIM)
    return o @ w_o

def swiglu(xn, w_gate, w_up, w_down):
    return (jax.nn.silu(xn @ w_gate) * (xn @ w_up)) @ w_down

def first_inputs(seed: int = 0) -> dict:
    key = jax.random.key(seed)
    ks = jax.random.split(key, 22)
    f32 = jnp.float32

    def nrm(k, shape, scale):
        return scale * jax.random.normal(k, shape, f32)

    def gain(k, shape):
        return 1.0 + 0.1 * jax.random.normal(k, shape, f32)

    return {
        "x": nrm(ks[0], (BATCH, SEQ, D_MODEL), 1.0),
        "mem": nrm(ks[1], (BATCH, MEM_LEN, D_MODEL), 1.0),
        "mix_norm_g": gain(ks[2], (DEPTH, D_MODEL)),
        "w_in": nrm(ks[3], (DEPTH, D_MODEL, IN_COLS), D_MODEL ** -0.5),
        "forget_bias": 4.0 + 0.5 * jax.random.normal(ks[4], (DEPTH, FOX_HEADS), f32),
        "conv_w": nrm(ks[5], (DEPTH, CONV_K, CONV_WIDTH), CONV_K ** -0.5),
        "sink": nrm(ks[6], (DEPTH, SWA_HEADS), 0.5),
        "w_branch": nrm(ks[7], (DEPTH, N_BRANCH, BRANCH_WIDTH, D_MODEL), BRANCH_WIDTH ** -0.5),
        "w_mix_out": nrm(ks[8], (DEPTH, D_MODEL, D_MODEL), D_MODEL ** -0.5),
        "rel_bias": nrm(ks[9], (N_BUCKETS, SWA_HEADS), 0.5),
        "xattn_norm_g": gain(ks[10], (DEPTH, D_MODEL)),
        "mem_norm_g": gain(ks[11], (DEPTH, D_MODEL)),
        "w_xq": nrm(ks[12], (DEPTH, D_MODEL, X_HEADS * X_HEAD_DIM), D_MODEL ** -0.5),
        "w_xkv": nrm(ks[13], (DEPTH, D_MODEL, 2 * X_HEADS * X_HEAD_DIM), D_MODEL ** -0.5),
        "w_xo": nrm(ks[14], (DEPTH, X_HEADS * X_HEAD_DIM, D_MODEL), (X_HEADS * X_HEAD_DIM) ** -0.5),
        "ffn_norm_g": gain(ks[15], (DEPTH, D_MODEL)),
        "w_ffn_gate": nrm(ks[16], (DEPTH, D_MODEL, D_FF), D_MODEL ** -0.5),
        "w_ffn_up": nrm(ks[17], (DEPTH, D_MODEL, D_FF), D_MODEL ** -0.5),
        "w_ffn_down": nrm(ks[18], (DEPTH, D_FF, D_MODEL), D_FF ** -0.5),
        "final_norm_g": gain(ks[19], (D_MODEL,)),
    }

def first_block(x, mem, mix_norm_g, w_in, forget_bias, conv_w, sink, w_branch, w_mix_out,
              rel_bias, xattn_norm_g, mem_norm_g, w_xq, w_xkv, w_xo, ffn_norm_g,
              w_ffn_gate, w_ffn_up, w_ffn_down, final_norm_g):
    b, s = x.shape[0], x.shape[1]
    for l in range(DEPTH):
        h = rms_norm(x, mix_norm_g[l])
        (c_b, c_c, c_u, f_q, f_k, f_v, f_g, s_q, s_k, s_v, gate_logits) = split_proj(h @ w_in[l])
        y_conv = short_conv_branch(c_b, c_c, c_u, conv_w[l])
        y_fox = fox_branch(f_q, f_k, f_v, f_g, forget_bias[l])
        y_swa = swa_sink_branch(s_q, s_k, s_v, rel_bias, sink[l])
        gates = jax.nn.sigmoid(gate_logits.reshape(b, s, N_BRANCH, D_MODEL))
        merged = (gates[:, :, 0] * (y_conv @ w_branch[l, 0])
                  + gates[:, :, 1] * (y_fox @ w_branch[l, 1])
                  + gates[:, :, 2] * (y_swa @ w_branch[l, 2]))
        x = x + merged @ w_mix_out[l]
        x = x + cross_attention(rms_norm(x, xattn_norm_g[l]), rms_norm(mem, mem_norm_g[l]),
                                w_xq[l], w_xkv[l], w_xo[l])
        x = x + swiglu(rms_norm(x, ffn_norm_g[l]), w_ffn_gate[l], w_ffn_up[l], w_ffn_down[l])
    return rms_norm(x, final_norm_g)


HG_HEADS = 8
HG_KEY_DIM = 128
HG_VAL_DIM = D_MODEL // HG_HEADS
HG_KEY = HG_HEADS * HG_KEY_DIM
HG_VAL = HG_HEADS * HG_VAL_DIM
HG_CHUNK = 64
SG_GROUPS = 8
SG_GROUP_DIM = 64
SG_WIDTH = SG_GROUPS * SG_GROUP_DIM
SG_CHUNK = 128
FFN_HIDDEN = ((8 * D_MODEL // 3 + 255) // 256) * 256
PLE_DIM = 256
EPS = 1e-6
IN_SPLITS = (HG_KEY, HG_KEY, HG_KEY, HG_VAL, HG_VAL, SG_WIDTH, SG_WIDTH, D_MODEL, D_MODEL)
N_IN = HG_KEY * 3 + HG_VAL * 2 + SG_WIDTH * 2 + D_MODEL * 2


def rms_norm_2(x, g):
    xf = x.astype(jnp.float32)
    y = xf * lax.rsqrt(jnp.mean(xf * xf, axis=-1, keepdims=True) + EPS)
    return (y * g.astype(jnp.float32)).astype(x.dtype)

def layer_norm(x, g, b):
    xf = x.astype(jnp.float32)
    mu = jnp.mean(xf, axis=-1, keepdims=True)
    xc = xf - mu
    y = xc * lax.rsqrt(jnp.mean(xc * xc, axis=-1, keepdims=True) + EPS)
    return (y * g.astype(jnp.float32) + b.astype(jnp.float32)).astype(x.dtype)

def layer_lower_bounds(gamma):
    sm = jax.nn.softmax(gamma.astype(jnp.float32), axis=0)
    return jnp.cumsum(sm, axis=0) - sm[0:1]

def _to_chunks(t):
    b, s, h, d = t.shape
    return t.reshape(b, s // HG_CHUNK, HG_CHUNK, h, d).transpose(1, 0, 3, 2, 4)

def hgrn2_direction(q, k, v, logf):
    bsz, s, h, dk = q.shape
    dv = v.shape[-1]
    mask = jnp.tril(jnp.ones((HG_CHUNK, HG_CHUNK), dtype=jnp.float32))

    def step(state, inp):
        qc, kc, vc, gc = inp
        b = jnp.cumsum(gc, axis=2)
        o_inter = jnp.einsum('bhtk,bhkv->bhtv', qc * jnp.exp(b), state)
        diff = b[:, :, :, None, :] - b[:, :, None, :, :]
        decay = jnp.exp(jnp.minimum(diff, 0.0)) * mask[:, :, None]
        scores = jnp.einsum('bhtk,bhsk,bhtsk->bhts', qc, kc, decay)
        o_intra = jnp.einsum('bhts,bhsv->bhtv', scores, vc)
        b_last = b[:, :, -1:, :]
        new_state = (jnp.exp(b_last[:, :, 0, :])[..., None] * state
                     + jnp.einsum('bhsk,bhsv->bhkv', kc * jnp.exp(b_last - b), vc))
        return new_state, o_inter + o_intra

    init = jnp.zeros((bsz, h, dk, dv), jnp.float32)
    _, o = lax.scan(step, init, (_to_chunks(q), _to_chunks(k), _to_chunks(v), _to_chunks(logf)))
    return o.transpose(1, 0, 3, 2, 4).reshape(bsz, s, h, dv)

def hgrn2_mixer(zq, zf_fwd, zf_bwd, zi, zg, lb_f, lb_b, norm_g):
    bsz, s, _ = zq.shape
    f32 = jnp.float32
    tiny = jnp.finfo(f32).tiny
    q = jax.nn.silu(zq.astype(f32)).reshape(bsz, s, HG_HEADS, HG_KEY_DIM)
    v = zi.astype(f32).reshape(bsz, s, HG_HEADS, HG_VAL_DIM)

    def gates(zf, lb):
        zf = zf.astype(f32)
        f = lb + (1.0 - lb) * jax.nn.sigmoid(zf)
        logf = jnp.log(jnp.maximum(f, tiny))
        k = (1.0 - lb) * jax.nn.sigmoid(-zf)
        return (k.reshape(bsz, s, HG_HEADS, HG_KEY_DIM), logf.reshape(bsz, s, HG_HEADS, HG_KEY_DIM))

    k_f, logf_f = gates(zf_fwd, lb_f)
    k_b, logf_b = gates(zf_bwd, lb_b)
    o_fwd = hgrn2_direction(q, k_f, v, logf_f)
    o_bwd = hgrn2_direction(q[:, ::-1], k_b[:, ::-1], v[:, ::-1], logf_b[:, ::-1])[:, ::-1]
    o = o_fwd + o_bwd
    o = rms_norm_2(o, norm_g.reshape(HG_HEADS, HG_VAL_DIM)).reshape(bsz, s, HG_VAL)
    return (o * jax.nn.silu(zg.astype(f32))).astype(zq.dtype)

def spatial_gating(zu, zv, w_s, b_s, ln_g, ln_b):
    bsz, s, _ = zu.shape
    u = jax.nn.gelu(zu, approximate=False)
    v = layer_norm(jax.nn.gelu(zv, approximate=False), ln_g, ln_b)
    vr = v.reshape(bsz, s // SG_CHUNK, SG_CHUNK, SG_GROUPS, SG_GROUP_DIM)
    sg = jnp.einsum('gts,bcsge->bctge', w_s, vr) + b_s.T[None, None, :, :, None]
    return u * sg.reshape(bsz, s, SG_WIDTH)

def second_inputs(seed: int = 0) -> dict:
    key = jax.random.key(seed)
    ks = jax.random.split(key, 24)
    f32 = jnp.float32

    def nrm(k, shape, scale):
        return jax.random.normal(k, shape, f32) * scale

    def gain(k, shape):
        return 1.0 + 0.05 * jax.random.normal(k, shape, f32)

    return {
        "x": nrm(ks[0], (BATCH, SEQ, D_MODEL), 1.0),
        "p": nrm(ks[1], (DEPTH, BATCH, SEQ, PLE_DIM), 1.0),
        "norm_mix_pre": gain(ks[2], (DEPTH, D_MODEL)),
        "w_in": nrm(ks[3], (DEPTH, D_MODEL, N_IN), D_MODEL ** -0.5),
        "lb_gamma_fwd": nrm(ks[4], (DEPTH, HG_KEY), 0.1),
        "lb_gamma_bwd": nrm(ks[5], (DEPTH, HG_KEY), 0.1),
        "hg_norm": gain(ks[6], (DEPTH, HG_VAL)),
        "sg_w": nrm(ks[7], (DEPTH, SG_GROUPS, SG_CHUNK, SG_CHUNK), SG_CHUNK ** -0.5),
        "sg_b": gain(ks[8], (DEPTH, SG_GROUPS, SG_CHUNK)),
        "sg_ln_g": gain(ks[9], (DEPTH, SG_WIDTH)),
        "sg_ln_b": nrm(ks[10], (DEPTH, SG_WIDTH), 0.02),
        "w_a": nrm(ks[11], (DEPTH, HG_VAL, D_MODEL), HG_VAL ** -0.5),
        "w_b": nrm(ks[12], (DEPTH, SG_WIDTH, D_MODEL), SG_WIDTH ** -0.5),
        "w_out": nrm(ks[13], (DEPTH, D_MODEL, D_MODEL), D_MODEL ** -0.5),
        "norm_mix_post": gain(ks[14], (DEPTH, D_MODEL)),
        "norm_ffn_pre": gain(ks[15], (DEPTH, D_MODEL)),
        "w_gate": nrm(ks[16], (DEPTH, D_MODEL, FFN_HIDDEN), D_MODEL ** -0.5),
        "w_up": nrm(ks[17], (DEPTH, D_MODEL, FFN_HIDDEN), D_MODEL ** -0.5),
        "w_down": nrm(ks[18], (DEPTH, FFN_HIDDEN, D_MODEL), FFN_HIDDEN ** -0.5),
        "norm_ffn_post": gain(ks[19], (DEPTH, D_MODEL)),
        "w_ple": nrm(ks[20], (DEPTH, PLE_DIM, D_MODEL), PLE_DIM ** -0.5),
        "w_ple_gate": nrm(ks[21], (DEPTH, D_MODEL, D_MODEL), D_MODEL ** -0.5),
    }

def second_block(x, p, norm_mix_pre, w_in, lb_gamma_fwd, lb_gamma_bwd, hg_norm, sg_w, sg_b,
              sg_ln_g, sg_ln_b, w_a, w_b, w_out, norm_mix_post, norm_ffn_pre, w_gate, w_up,
              w_down, norm_ffn_post, w_ple, w_ple_gate):
    lb_fwd_all = layer_lower_bounds(lb_gamma_fwd)
    lb_bwd_all = layer_lower_bounds(lb_gamma_bwd)
    offsets = [int(o) for o in np.cumsum(IN_SPLITS)[:-1]]
    for l in range(DEPTH):
        h = rms_norm_2(x, norm_mix_pre[l])
        z = jnp.einsum('bsd,dn->bsn', h, w_in[l])
        zq, zf_f, zf_b, zi, zg, zu, zv, ga, gb = jnp.split(z, offsets, axis=-1)
        a_out = hgrn2_mixer(zq, zf_f, zf_b, zi, zg, lb_fwd_all[l], lb_bwd_all[l], hg_norm[l])
        b_out = spatial_gating(zu, zv, sg_w[l], sg_b[l], sg_ln_g[l], sg_ln_b[l])
        merged = (jax.nn.sigmoid(ga) * jnp.einsum('bsv,vd->bsd', a_out, w_a[l])
                  + jax.nn.sigmoid(gb) * jnp.einsum('bsw,wd->bsd', b_out, w_b[l]))
        mix = jnp.einsum('bsd,de->bse', merged, w_out[l])
        x = x + rms_norm_2(mix, norm_mix_post[l])
        h2 = rms_norm_2(x, norm_ffn_pre[l])
        ff = jnp.einsum('bsf,fd->bsd',
                        jax.nn.silu(jnp.einsum('bsd,df->bsf', h2, w_gate[l]))
                        * jnp.einsum('bsd,df->bsf', h2, w_up[l]), w_down[l])
        x = x + rms_norm_2(ff, norm_ffn_post[l])
        x = x + (jnp.einsum('bse,ed->bsd', p[l], w_ple[l])
                 * jax.nn.sigmoid(jnp.einsum('bsd,de->bse', x, w_ple_gate[l])))
    return x


def setup_inputs(seed=0):
    out = dict(first_inputs(seed))
    for name, value in second_inputs(seed + 1).items():
        if name != "x":
            out[name + "_2"] = value
    return out


def reference(
    x, mem, mix_norm_g, w_in, forget_bias, conv_w, sink, w_branch, w_mix_out, rel_bias,
    xattn_norm_g, mem_norm_g, w_xq, w_xkv, w_xo, ffn_norm_g, w_ffn_gate, w_ffn_up, w_ffn_down,
    final_norm_g, p_2, norm_mix_pre_2, w_in_2, lb_gamma_fwd_2, lb_gamma_bwd_2, hg_norm_2,
    sg_w_2, sg_b_2, sg_ln_g_2, sg_ln_b_2, w_a_2, w_b_2, w_out_2, norm_mix_post_2,
    norm_ffn_pre_2, w_gate_2, w_up_2, w_down_2, norm_ffn_post_2, w_ple_2, w_ple_gate_2,
):
    x = first_block(
        x, mem, mix_norm_g, w_in, forget_bias, conv_w, sink, w_branch, w_mix_out, rel_bias,
        xattn_norm_g, mem_norm_g, w_xq, w_xkv, w_xo, ffn_norm_g, w_ffn_gate, w_ffn_up,
        w_ffn_down, final_norm_g,
    )
    return second_block(
        x, p_2, norm_mix_pre_2, w_in_2, lb_gamma_fwd_2, lb_gamma_bwd_2, hg_norm_2, sg_w_2,
        sg_b_2, sg_ln_g_2, sg_ln_b_2, w_a_2, w_b_2, w_out_2, norm_mix_post_2, norm_ffn_pre_2,
        w_gate_2, w_up_2, w_down_2, norm_ffn_post_2, w_ple_2, w_ple_gate_2,
    )


_drawn_inputs = setup_inputs


def setup_inputs(seed=0):
    import zlib

    import numpy as np

    out = dict(_drawn_inputs(seed))
    spreads = {}
    factors = {'sink': 7.578,
     'xattn_norm_g': 4.187,
     'mem_norm_g': 2.726,
     'hg_norm_2': 2.713,
     'sg_ln_g_2': 2.677,
     'sg_ln_b_2': 5.68}
    for name, (base, spread) in spreads.items():
        noise = np.random.default_rng([zlib.crc32(name.encode()), seed]).standard_normal(out[name].shape)
        drawn = base * np.exp(spread * noise) if base else spread * noise
        out[name] = jnp.asarray(drawn.astype(out[name].dtype))
    for name, factor in factors.items():
        out[name] = (out[name] * factor).astype(out[name].dtype)
    return out
```

```python
import numpy as np
import concourse.bass as bass
from concourse import mybir

F32 = mybir.dt.float32
F32R = mybir.dt.float32r
U8 = mybir.dt.uint8
ALU = mybir.AluOpType
ACT = mybir.ActivationFunctionType
X_AXIS = mybir.AxisListType.X

P = 128
T = 256
EPS = 1e-6
NEG = -1e30
KB = 1024
BASE = 16896
UNIT = 2048
RAW = 3
SPLIT = 3
LEVELS = [1, 2, 4, 8, 16, 32, 64]

G_ROWS = [("mix_norm_g", 8), ("xattn_norm_g", 8), ("mem_norm_g", 8), ("ffn_norm_g", 8), ("final_norm_g", 8),
          ("norm_mix_pre_2", 8), ("norm_mix_post_2", 8), ("norm_ffn_pre_2", 8), ("norm_ffn_post_2", 8),
          ("hg_norm_2", 8), ("conv_w", 12), ("lb_gamma_fwd_2", 8), ("lb_gamma_bwd_2", 8)]
G_AT = {}
for _name, _n in G_ROWS:
    G_AT[_name] = sum(n for x, n in G_ROWS[:[g[0] for g in G_ROWS].index(_name)])
G_N = sum(n for _, n in G_ROWS)


def constants():
    i = np.arange(P)
    ident = np.eye(P, dtype=np.float32)
    causal = np.where(i[None, :] <= i[:, None], 0.0, NEG).astype(np.float32)
    big = np.concatenate([ident, causal, np.zeros((P, P), np.float32), causal], axis=1)
    masks = []
    for h in LEVELS:
        same = (i[:, None] // (2 * h)) == (i[None, :] // (2 * h))
        other = (i[:, None] // h) != (i[None, :] // h)
        masks.append((same & other).astype(np.float32))
    masks = np.concatenate(masks, axis=1)
    dist = 255 - np.arange(384)
    inside = (dist >= 0) & (dist < 128)
    n = np.maximum(dist, 1).astype(np.float32)
    large = 16 + (np.log(n / np.float32(16)) / np.float32(np.log(8.0)) * np.float32(16)).astype(np.int32)
    bucket = np.where(dist < 16, np.maximum(dist, 0), np.minimum(large, 31))
    small = np.zeros((32, 896), np.float32)
    small[:, 0:384] = (np.arange(32)[:, None] == bucket[None, :]) & inside[None, :]
    small[0:8, 384:768] = np.where(inside, 0.0, NEG)[None, :]
    for r in range(16):
        second = float(r >= 8)
        small[r, 768] = second
        small[r, 769] = -(1.0 - second)
        small[r, 776 + r % 8] = 1.0 - second
        small[r, 784 + r % 8] = second
    return {"c_big": big, "c_masks": masks, "c_small": small}


class Line:

    def __init__(self, sem):
        self.sem, self.n, self.items, self.seen = sem, 0, [], {}

    def waits(self, after):
        need = {}
        for token in after:
            if token is None:
                continue
            if isinstance(token, list):
                for s, v in self.waits(token):
                    need[s] = max(need.get(s, 0), v)
                continue
            s, v = token
            need[s] = max(need.get(s, 0), v)
        return list(need.items())

    def do(self, ins, *after, mark=True):
        for s, v in self.waits(list(after)):
            if self.seen.get(s, 0) < v:
                self.seen[s] = v
                self.items.append(("wait", s, v))
        self.items.append(("do", ins, mark))
        if mark:
            self.n += 1
            return (self.sem, self.n)
        return None

    def replay(self, eng):
        for what, a, b in self.items:
            if what == "wait":
                eng.wait_ge(a, b)
            else:
                done = a(eng)
                if b:
                    done.then_inc(self.sem, 1)


class Loads:

    def __init__(self, line):
        self.line = line

    def go(self, sem, value, out, in_, *after):
        self.line.do(lambda e, o=out, i=in_, s=sem: e.dma_start(o, i).then_inc(s, 16), *after, mark=False)
        return (sem, value)


def build(nc, d, out):
    def at(name, shape, dt, kb):
        return nc.alloc_sbuf_tensor_at(name, shape, dt, offset=BASE + int(kb * KB))

    def sem(name):
        return nc.alloc_semaphore(name)

    def flat(ap):
        return ap

    raw = [at(f"raw{i}", [P, UNIT], F32, 8 * i) for i in range(RAW)]
    whi = [at(f"whi{i}", [P, UNIT], F32R, 24 + 8 * i) for i in range(SPLIT)]
    wlo = [at(f"wlo{i}", [P, UNIT], F32R, 48 + 8 * i) for i in range(SPLIT)]
    HA = (at("ha_hi", [P, 8, T], F32R, 72), at("ha_lo", [P, 8, T], F32R, 80))
    GC = at("gc", [P, P], F32, 88)
    ident = at("ident", [P, P], F32, 88.5)
    ones = at("ones", [P, P], F32, 89)
    M3 = at("m3", [P, 384], F32, 89.5)
    masks = at("masks", [P, 7, 512], U8, 91)
    sc = at("sc", [P, 256], F32, 94.5)
    zero = sc[:, 0:1]
    epsc = sc[:, 1:2]

    X = at("xres", [P, 8, T], F32, 96)
    x_tm = at("x_tm", [P, 2, 1024], F32, 96)
    m_tm = at("m_tm", [P, 2, 1024], F32, 104)
    n_tm = at("n_tm", [P, 2, 1024], F32, 112)
    n_t = [at(f"n_t{i}", [P, 4, T], F32, 120 + 4 * i) for i in range(2)]
    MN = (at("mn_hi", [P, 8, T], F32R, 128), at("mn_lo", [P, 8, T], F32R, 136))
    xK = at("xk", [P, 8, T], F32, 144)
    xV = at("xv", [P, 2, 1024], F32, 152)
    gates = at("gates", [P, 24, T], F32, 160)
    fq = at("fq", [P, 4, T], F32, 184)
    fk = at("fk", [P, 4, T], F32, 188)
    fv = at("fv", [P, 2, 512], F32, 192)
    sq_ = at("sq", [P, 4, T], F32, 196)
    sk = at("sk", [P, T], F32, 200)
    sv = at("sv", [P, 2, 128], F32, 201)
    cA = [at(f"ca{i}", [16, T], F32, 202 + i) for i in range(2)]
    cB = [at(f"cb{i}", [16, T], F32, 204 + i) for i in range(2)]
    z = at("z", [P, 4, T], F32, 96)
    cc = at("cc", [P, 4, T], F32, 100)
    YH = at("y_hi", [P, 12, T], F32R, 104)
    YL = at("y_lo", [P, 12, T], F32R, 116)
    bias = at("bias", [P, 8, 256], F32, 128)
    Lb = [at(f"lb{i}", [P, 384], F32, 136 + 1.5 * i) for i in range(2)]
    PT = [at(f"pt{i}", [P, 384], F32, 139 + 1.5 * i) for i in range(2)]
    ot = [at(f"ot{i}", [P, T], F32, 142 + i) for i in range(2)]
    small = at("small", [32, 896], F32, 112)
    bt = at("bt", [8, 384], F32, 116)
    mg = [at(f"mg{i}", [P, 4, T], F32, 184 + 4 * i) for i in range(2)]
    mt = at("mt", [P, 4, T], F32, 192)
    MG = (at("mg_hi", [P, 8, T], F32R, 128), at("mg_lo", [P, 8, T], F32R, 136))
    x_tm2 = at("x_tm2", [P, 2, 1024], F32, 196)
    nsq = at("nsq", [P, 8, T], F32, 164)
    nrs = at("nrs", [P, T], F32, 172)
    nh = at("nh", [P, 8, T], F32, 174)
    xq = at("xq", [P, 8, T], F32, 184)
    xL = [at(f"xl{i}", [P, 2, T], F32, 192 + 2 * i) for i in range(2)]
    xPT = [at(f"xpt{i}", [P, 2, T], F32, 196 + 2 * i) for i in range(2)]
    xo = [at(f"xo{i}", [P, 2, T], F32, 200 + 2 * i) for i in range(2)]
    OX = (at("ox_hi", [P, 8, T], F32R, 104), at("ox_lo", [P, 8, T], F32R, 112))
    PR = (at("pr_hi", [P, 22, T], F32R, 104), at("pr_lo", [P, 22, T], F32R, 126))
    silu = [at(f"silu{i}", [P, 1024], F32, 148 + 4 * i) for i in range(2)]
    prod = [at(f"prod{i}", [P, 1024], F32, 156 + 4 * i) for i in range(2)]

    v = at("v", [P, 2, 1024], F32, 104)
    q = at("q", [P, 4, T], F32, 112)
    kf = at("kf", [P, 4, T], F32, 116)
    kb = at("kb", [P, 4, T], F32, 120)
    Pf = at("pf", [P, 4, T], F32, 124)
    Xf = at("xf", [P, 4, T], F32, 128)
    Pb = at("pb", [P, 4, T], F32, 132)
    Xb = at("xb", [P, 4, T], F32, 136)
    Qt = [at(f"qt{i}", [P, 4, T], F32, 140 + 4 * i) for i in range(2)]
    Kt = [at(f"kt{i}", [P, 4, T], F32, 148 + 4 * i) for i in range(2)]
    Am = at("am", [P, 4, 2, T], F32, 156)
    zv = at("zv", [P, 2, 512], F32, 140)
    zu = at("zu", [P, 4, T], F32, 144)
    wsT = at("wst", [P, 8, P], F32, 148)
    ws = at("ws", [P, 8, P], F32, 152)
    bsb = at("bsb", [P, 4, P], F32, 156)
    lng = at("lng", [P, 512], F32, 158)
    lnb = at("lnb", [P, 512], F32, 160)
    BO = (at("bo_hi", [P, 4, T], F32R, 188), at("bo_lo", [P, 4, T], F32R, 192))
    bo = at("bo", [P, 4, T], F32, 196)
    zg = at("zg", [P, 8, T], F32, 164)
    ga = at("ga", [P, 8, T], F32, 172)
    gb = at("gb", [P, 8, T], F32, 180)
    AO = (at("ao_hi", [P, 8, T], F32R, 188), at("ao_lo", [P, 8, T], F32R, 196))
    ho = at("ho", [P, 4, T], F32, 156 - 16)
    hs = at("hs", [P, 4, T], F32, 156 - 12)
    hr = at("hr", [P, 4, T], F32, 156 - 8)
    ML = (at("ml_hi", [P, 8, T], F32R, 104), at("ml_lo", [P, 8, T], F32R, 112))
    mtmp = [at(f"mtmp{i}", [P, 4, T], F32, 128 + 4 * i) for i in range(2)]
    mix = at("mix", [P, 8, T], F32, 182)
    p_tm = at("p_tm", [P, 2, 256], F32, 190)
    PL = (at("pl_hi", [P, 2, T], F32R, 194), at("pl_lo", [P, 2, T], F32R, 196))
    pt32 = at("pt32", [P, 2, T], F32, 192)
    tg = [at(f"tg{i}", [P, 4, T], F32, 148 + 4 * i) for i in range(2)]
    pp = at("pp", [P, 8, T], F32, 156)
    y_tm = at("y_tm", [P, 2, 1024], F32, 104)

    banks = [nc.alloc_psum_tensor(f"ps{i}", [P, 1024], F32) for i in range(4)]
    scratch = nc.dram_tensor("rel_rows", [8, P, 384], F32)
    scr = scratch.ap()

    pe, act, dve, pool, sp = (Line(sem(f"s_{n}")) for n in ("pe", "act", "dve", "pool", "sp"))
    queue = Loads(sp)
    misc = [0]

    def load(out_, in_, *after):
        misc[0] += 1
        return queue.go(sem(f"s_ld{misc[0]}"), 16, out_, in_, *after)

    class Weights:
        def __init__(self):
            self.units = []
            self.sems = [sem(f"s_w{i}") for i in range(RAW)]
            self.fills = [0] * RAW
            self.loaded, self.split, self.used, self.raws = {}, {}, {}, 0
            self.done = 0

        def add(self, parts, nk, ncol):
            self.units.append((parts, nk, ncol))
            return len(self.units) - 1

        def fetch(self, n):
            parts, nk, ncol = self.units[n]
            slot = n % RAW
            after = [self.split[n - RAW]] if n >= RAW else []
            for where, src in parts:
                self.fills[slot] += 16
                queue.go(self.sems[slot], self.fills[slot], where(raw[slot][:, 0:nk * ncol]), src, *after)
            self.loaded[n] = (self.sems[slot], self.fills[slot])

        def prepare(self, n):
            while self.raws < min(n + RAW, len(self.units)) and (
                    self.raws < RAW or self.raws - RAW in self.split):
                self.fetch(self.raws)
                self.raws += 1
            parts, nk, ncol = self.units[n]
            size = nk * ncol
            r, h, l = raw[n % RAW][:, 0:size], whi[n % SPLIT][:, 0:size], wlo[n % SPLIT][:, 0:size]
            free = self.used.get(n - SPLIT)
            a = act.do(lambda e: e.activation(h, r, ACT.Copy), self.loaded[n], free)
            line = pool if n % 4 == 3 else dve
            self.split[n] = line.do(lambda e: e.tensor_tensor(l, r, h.bitcast(F32), ALU.subtract), a, self.loaded[n], free)
            if self.raws < len(self.units) and self.raws - RAW in self.split:
                self.fetch(self.raws)
                self.raws += 1

        def ahead(self, n):
            while self.done <= min(n, len(self.units) - 1):
                self.prepare(self.done)
                self.done += 1

        def take(self, n):
            self.ahead(n + SPLIT - 1)
            parts, nk, ncol = self.units[n]
            view = "p (k n) -> p k n"
            return (whi[n % SPLIT][:, 0:nk * ncol].rearrange(view, k=nk),
                    wlo[n % SPLIT][:, 0:nk * ncol].rearrange(view, k=nk), self.split[n])

    W = Weights()

    def cols(w, c0_, n, nk_total, step=None):
        step = step or UNIT // n
        view = w.rearrange("(k p) n -> p k n", p=P)
        got = []
        for k0 in range(0, nk_total, step):
            nk = min(step, nk_total - k0)
            dst = lambda r, nk=nk: r.rearrange("p (k n) -> p k n", k=nk)
            got.append((W.add([(dst, view[:, k0:k0 + nk, c0_:c0_ + n])], nk, n), k0, nk))
        return got

    state = {"sets": [0, 1], "turn": 0}
    free = {i: None for i in range(4)}

    def next_set():
        s = state["sets"][state["turn"] % len(state["sets"])]
        state["turn"] += 1
        return s

    bg = []

    def tick():
        if bg:
            try:
                next(bg[0])
            except StopIteration:
                bg.pop(0)

    def passes(hi_w, lo_w, hi_x, lo_x):
        return [(hi_w, hi_x), (hi_w, lo_x), (lo_w, hi_x)]

    def linear(units, H, nm, ready, width=P):
        s = next_set()
        ps = banks[s]
        K = units[-1][1] + units[-1][2]
        hi_x, lo_x, off = H
        tok = None
        for u, k0, nk in units:
            wh, wl, wt = W.take(u)
            for m in range(nm):
                for kk in range(nk):
                    k = k0 + kk
                    for j, (a, b) in enumerate(passes(wh, wl, hi_x, lo_x)):
                        first = k == 0 and j == 0
                        last = k == K - 1 and j == 2
                        tok = pe.do(lambda e, a=a, b=b, m=m, kk=kk, k=k, first=first, last=last: e.matmul(
                            ps[0:width, m * T:(m + 1) * T], a[:, kk, m * width:(m + 1) * width], b[:, off + k, :],
                            start=first and m % 2 == 0, stop=last, skip_group_check=True),
                            wt, ready[k] if isinstance(ready, dict) else ready, free[s],
                            mark=(m == nm - 1 and kk == nk - 1 and j == 2))
            W.used[u] = tok
            tick()
        return s, tok

    def linear_tm(units, H, ncol, c_in, ready):
        s = next_set()
        ps = banks[s]
        K = units[-1][1] + units[-1][2]
        hi_x, lo_x, off = H
        for u, k0, nk in units:
            wh, wl, wt = W.take(u)
            for t in range(2):
                for kk in range(nk):
                    k = k0 + kk
                    for j, (a, b) in enumerate(passes(wh, wl, hi_x, lo_x)):
                        tok = pe.do(lambda e, a=a, b=b, t=t, kk=kk, k=k, j=j: e.matmul(
                            ps[:, t * 512:t * 512 + ncol], b[:, off + k, t * P:(t + 1) * P],
                            a[:, kk, c_in:c_in + ncol],
                            start=(k == 0 and j == 0), stop=(k == K - 1 and j == 2), skip_group_check=True),
                            wt, ready, free[s], mark=(t == 1 and kk == nk - 1 and j == 2))
            W.used[u] = tok
            tick()
        return s, tok

    def split(hi, lo, src, *after, line=None, scale=1.0):
        a = act.do(lambda e: e.activation(hi, src, ACT.Copy, scale=scale), *after)
        line = line or dve
        if scale == 1.0:
            return line.do(lambda e: e.tensor_tensor(lo, src, hi.bitcast(F32), ALU.subtract), a, *after)
        return dve.do(lambda e: e.scalar_tensor_tensor(out=lo, in0=src, scalar=scale, in1=hi.bitcast(F32),
                                                       op0=ALU.mult, op1=ALU.subtract), a, *after)

    def g_col(name, k):
        return GC[:, G_AT[name] + k:G_AT[name] + k + 1]

    g_tm = at("g_tm", [P, P], F32, 144)
    g_loads = []
    for name, n in G_ROWS:
        src = d[name]
        src = src.rearrange("a b n -> (a b) n") if len(src.shape) == 3 else src
        if len(src.shape) == 2:
            src = src.rearrange("a (k p) -> (a k) p", p=P)
        else:
            src = src.rearrange("(k p) -> k p", p=P)
        g_loads.append((name, n, src))
    t_x = load(x_tm[:, :, :], d["x"].rearrange("a (t p) n -> p (a t) n", p=P))
    t_m = load(m_tm[:, :, :], d["mem"].rearrange("a (t p) n -> p (a t) n", p=P))
    t_id = load(ident[:, :], d["c_big"][:, 0:128])
    t_m3 = load(M3[:, :], d["c_big"][:, 128:512])
    gsem = sem("s_g")
    t_g = None
    for i, (name, n, src) in enumerate(g_loads):
        t_g = queue.go(gsem, 16 * (i + 1), g_tm[G_AT[name]:G_AT[name] + n, :], src)
    sinkc = sc[:, 8:16]
    t_sink = load(sinkc, d["sink"].partition_broadcast(P).rearrange("p a n -> p (a n)"))
    fb = sc[0:16, 16:17]
    fbsem = sem("s_fb")
    queue.go(fbsem, 16, sc[0:8, 16:17], d["forget_bias"].rearrange("a n -> n a"))
    t_fb = queue.go(fbsem, 32, sc[8:16, 16:17], d["forget_bias"].rearrange("a n -> n a"))
    mk = at("mk", [P, 7, P], F32, 152)
    t_mk = load(mk[:, :, :], d["c_masks"].rearrange("p (l n) -> p l n", l=7))
    t_ms = dve.do(lambda e: e.tensor_copy(masks[:, :, :].rearrange("p l (m n) -> p l m n", m=4),
                                          mk[:, :, :].unsqueeze(2).broadcast_to([P, 7, 4, P])), t_mk)
    t_eps = dve.do(lambda e: e.memset(sc[:, 1:2], EPS))
    t_zero = dve.do(lambda e: e.memset(sc[:, 0:1], 0.0))
    t_one = dve.do(lambda e: e.memset(ones[:, :], 1.0))

    w_in = d["w_in"].rearrange("a k n -> (a k) n")
    U = {}
    w_kv = d["w_xkv"].rearrange("a k n -> (a k) n")
    U["mk"] = [cols(w_kv, 512 * i, 512, 8) for i in range(2)]
    U["mv"] = [cols(w_kv, 1024 + 512 * i, 512, 8) for i in range(2)]
    U["fq"] = cols(w_in, 1536, 512, 8)
    U["fk"] = cols(w_in, 2048, 512, 8)
    U["fv"] = cols(w_in, 2560, 512, 8)
    fg_v = w_in.rearrange("(k p) n -> p k n", p=P)[:, :, 3072:3080]
    U["fg"] = [(W.add([(lambda r: r.rearrange("p (k n) -> p k n", k=8)[:, :, 0:8], fg_v),
                       (lambda r: r.rearrange("p (k n) -> p k n", k=8)[:, :, 8:16], fg_v)], 8, 16), 0, 8)]
    sqv = w_in.rearrange("(k p) n -> p k n", p=P)[:, :, 3080:3592].rearrange("p k (u j c) -> p k u j c", u=2, j=4)
    U["sq"] = []
    for k0 in (0, 4):
        parts = []
        for kk in range(4):
            for u in range(2):
                dst = (lambda r, u=u, kk=kk: r.rearrange("p (k j u c) -> p k j u c", k=4, j=4, u=2)[:, kk, :, u, :])
                parts.append((dst, sqv[:, k0 + kk, u, :, :]))
        U["sq"].append((W.add(parts, 4, 512), k0, 4))
    U["skv"] = cols(w_in, 3592, 256, 8)
    U["cc"] = cols(w_in, 512, 512, 8)
    U["cu"] = cols(w_in, 1024, 512, 8)
    U["cb"] = cols(w_in, 0, 512, 8)
    U["gates"] = [cols(w_in, 3848 + 512 * i, 512, 8) for i in range(6)]
    wb = d["w_branch"].rearrange("a b k n -> (a b) k n")
    U["br"] = []
    for g in range(2):
        U["br"].append(cols(wb[0], 512 * g, 512, 4))
        U["br"].append(cols(wb[1], 512 * g, 512, 4))
        wv = wb[2].rearrange("(u j p) n -> u p j n", u=2, j=4)
        parts = [((lambda r, u=u: r[64 * u:64 * u + 64, :].rearrange("p (k n) -> p k n", k=4)),
                  wv[u][:, :, 512 * g:512 * g + 512]) for u in range(2)]
        U["br"].append([(W.add(parts, 4, 512), 0, 4)])

    def pair(name, n_groups, k):
        w = d[name].rearrange("a k n -> (a k) n")
        return [cols(w, 512 * i, 512, k) for i in range(n_groups)]

    U["mo"] = pair("w_mix_out", 2, 8)
    U["xq"] = pair("w_xq", 2, 8)
    U["xo"] = pair("w_xo", 2, 8)

    def ffn_units(gate, up, down):
        wg = d[gate].rearrange("a k n -> (a k) n")
        wu = d[up].rearrange("a k n -> (a k) n")
        got = []
        for i in range(6):
            n = 512 if i < 5 else 256
            got.append((cols(wg, 512 * i, n, 8), cols(wu, 512 * i, n, 8)))
        return got, pair(down, 2, 22)

    U["ffn1"] = ffn_units("w_ffn_gate", "w_ffn_up", "w_ffn_down")
    w2 = d["w_in_2"].rearrange("a k n -> (a k) n")
    U["zv"] = cols(w2, 5632, 512, 8)
    U["zu"] = cols(w2, 5120, 512, 8)

    def half_units(i):
        return {"ff": cols(w2, 1024 + 512 * i, 512, 8), "fb": cols(w2, 2048 + 512 * i, 512, 8),
                "q": cols(w2, 512 * i, 512, 8)}

    U["h0"] = half_units(0)
    U["zi"] = [cols(w2, 3072 + 512 * i, 512, 8) for i in range(2)]
    U["gb"] = [cols(w2, 7168 + 512 * i, 512, 8) for i in range(2)]
    U["wb2"] = pair("w_b_2", 2, 4)
    U["zg"] = [cols(w2, 4096 + 512 * i, 512, 8) for i in range(2)]
    U["h1"] = half_units(1)
    U["ga"] = [cols(w2, 6144 + 512 * i, 512, 8) for i in range(2)]
    U["wa2"] = pair("w_a_2", 2, 8)
    U["wo2"] = pair("w_out_2", 2, 8)
    U["ffn2"] = ffn_units("w_gate_2", "w_up_2", "w_down_2")
    U["ple"] = pair("w_ple_2", 2, 2)
    U["pg"] = pair("w_ple_gate_2", 2, 8)

    W.ahead(1)

    s = next_set()
    t = pe.do(lambda e: e.transpose(banks[s][:, 0:G_N], g_tm[0:G_N, :], ident[0:G_N, 0:G_N]), t_g, t_id, free[s])
    t_gc = dve.do(lambda e, s=s: e.tensor_copy(GC[:, 0:G_N], banks[s][:, 0:G_N]), t)
    free[s] = t_gc

    def rs_tm(src, col, junk, *after):
        for t_ in range(2):
            a = act.do(lambda e, t_=t_: e.activation(junk[:, t_, :], src[:, t_, :], ACT.Square,
                                                     accum_out=sc[:, col + t_:col + t_ + 1]), *after)
        a = act.do(lambda e: e.activation(sc[:, col:col + 2], sc[:, col:col + 2], ACT.Ln, bias=epsc,
                                          scale=1.0 / 1024), a, t_eps)
        return act.do(lambda e: e.activation(sc[:, col:col + 2], sc[:, col:col + 2], ACT.Exp, bias=zero,
                                             scale=-0.5), a, t_zero)

    def norm_tm(src, col, H, gname, t_src, *after):
        t_rs = rs_tm(src, col, n_tm, t_src, *after)
        for t_ in range(2):
            t_h = dve.do(lambda e, t_=t_: e.tensor_scalar(n_tm[:, t_, :], src[:, t_, :],
                                                          sc[:, col + t_:col + t_ + 1], None, ALU.mult), t_rs)
        ready = {}
        for g in range(2):
            s = next_set()
            for k in range(4):
                for t_ in range(2):
                    tp = pe.do(lambda e, k=k, t_=t_, g=g, s=s: e.transpose(
                        banks[s][:, k * T + t_ * P:k * T + t_ * P + P], n_tm[:, t_, (4 * g + k) * P:(4 * g + k + 1) * P],
                        ident[:, :]), t_h, t_id, free[s], mark=(k == 3 and t_ == 1))
            for k in range(4):
                te = dve.do(lambda e, k=k, g=g, s=s: e.tensor_scalar(
                    n_t[g][:, k, :], banks[s][:, k * T:(k + 1) * T], g_col(gname, 4 * g + k), None, ALU.mult),
                    tp, t_gc, norm_tm.last[g])
            free[s] = te
            tok = split(H[0][:, 4 * g:4 * g + 4, :], H[1][:, 4 * g:4 * g + 4, :], n_t[g][:, :, :], te)
            norm_tm.last[g] = tok
            for k in range(4):
                ready[4 * g + k] = tok
        return ready, tp

    norm_tm.last = [None, None]
    r_m, tp_m = norm_tm(m_tm, 20, MN, "mem_norm_g", t_m)
    r_h, tp_h = norm_tm(x_tm, 22, HA, "mix_norm_g", t_x, tp_m)
    t_hx = r_h[7]

    for i in range(2):
        s, tk = linear(U["mk"][i], MN + (0,), 4, r_m)
        free[s] = act.do(lambda e, i=i, s=s: e.activation(
            xK[:, 4 * i:4 * i + 4, :], banks[s][:, :], ACT.Copy), tk)
    t_xK = free[s]
    for i in range(2):
        s, tk = linear_tm(U["mv"][i], MN + (0,), 512, 0, r_m[7])
        free[s] = act.do(lambda e, i=i, s=s: e.activation(
            xV[:, :, 512 * i:512 * i + 512], banks[s][:, :].rearrange("p (t n) -> p t n", t=2), ACT.Copy), tk, t_ms)
    t_xV = free[s]
    t_mem_done = tk

    t_sm = load(small[:, :], d["c_small"], t_mem_done, tp_h)
    relb = sc[0:32, 32:40]
    t_rb = load(relb, d["rel_bias"])
    s = next_set()
    tk = pe.do(lambda e, s=s: e.matmul(banks[s][0:8, 0:384], relb, small[:, 0:384], start=True, stop=True),
               t_sm, t_rb, free[s])
    free[s] = dve.do(lambda e, s=s: e.tensor_tensor(bt[:, :], banks[s][0:8, 0:384], small[0:8, 384:768], ALU.add), tk)
    t_scr = load(scr, bt[:, :].unsqueeze(1).broadcast_to([8, P, 384]), free[s])
    rows = bass.AP(scratch, 127, [[383, 128], [P * 384, 8], [1, 256]])
    t_bias = load(bias[:, :, :], rows, t_scr, t_mem_done)
    sel = sc[0:16, 40:64]
    t_sel = dve.do(lambda e: e.tensor_copy(sel, small[0:16, 768:792]), t_sm)

    H = HA + (0,)
    s, tk = linear(U["fq"], H, 4, r_h)
    free[s] = act.do(lambda e, s=s: e.activation(fq[:, :, :], banks[s][:, :], ACT.Copy, scale=0.125), tk)
    t_fq = free[s]
    s, tk = linear(U["fk"], H, 4, r_h)
    t_fk = free[s] = act.do(lambda e, s=s: e.activation(fk[:, :, :], banks[s][:, :], ACT.Copy), tk)
    s, tk = linear_tm(U["fv"], H, 512, 0, t_hx)
    t_fv = free[s] = act.do(lambda e, s=s: e.activation(
        fv[:, :, :], banks[s][:, :].rearrange("p (t n) -> p t n", t=2), ACT.Copy), tk)
    s, tk = linear(U["fg"], H, 1, r_h, width=16)
    la, lb_ = cA, cB
    t1 = free[s] = dve.do(lambda e, s=s: e.tensor_scalar(la[0][:, :], banks[s][0:16, 0:T], fb, None, ALU.add), tk, t_fb)
    t2 = act.do(lambda e: e.activation(la[1][:, :], la[0][:, :], ACT.Abs), t1)
    t2 = act.do(lambda e: e.activation(la[1][:, :], la[1][:, :], ACT.Exp, bias=zero[0:16, :], scale=-1.0), t2)
    t2 = act.do(lambda e: e.activation(la[1][:, :], la[1][:, :], ACT.Ln, bias=1.0), t2)
    t3 = dve.do(lambda e: e.tensor_scalar(lb_[0][:, :], la[0][:, :], 0.0, None, ALU.min), t1)
    t3 = dve.do(lambda e: e.tensor_tensor(lb_[1][:, :], lb_[0][:, :], la[1][:, :], ALU.subtract), t2, t3)
    cur, step = lb_[1], 1
    bufs = [lb_[0], lb_[1]]
    while step < T:
        nxt = bufs[0] if cur is bufs[1] else bufs[1]
        t4 = dve.do(lambda e, a=cur, b=nxt, n=step: e.tensor_copy(b[:, 0:n], a[:, 0:n]), t3)
        t3 = dve.do(lambda e, a=cur, b=nxt, n=step: e.tensor_tensor(b[:, n:T], a[:, n:T], a[:, 0:T - n], ALU.add), t3)
        cur, step = nxt, step * 2
    cumc = at("cumc", [16, T], F32, 206)
    t_c = dve.do(lambda e, a=cur: e.tensor_copy(cumc[:, :], a[:, :]), t3, t4)

    s, tk = linear(U["sq"], H, 4, r_h)
    t_sq = free[s] = act.do(lambda e, s=s: e.activation(sq_[:, :, :], banks[s][:, :], ACT.Copy, scale=0.125), tk)
    u, k0, nk = U["skv"][0]
    s = next_set()
    ps = banks[s]
    wh, wl, wt = W.take(u)
    for k in range(8):
        for j, (a, b) in enumerate(passes(wh, wl, HA[0], HA[1])):
            pe.do(lambda e, a=a, b=b, k=k, j=j, ps=ps: e.matmul(
                ps[:, 0:T], a[:, k, 0:P], b[:, k, :], start=(k == 0 and j == 0), stop=(k == 7 and j == 2),
                skip_group_check=True), wt, t_hx, free[s], mark=False)
    for t_ in range(2):
        for k in range(8):
            for j, (a, b) in enumerate(passes(wh, wl, HA[0], HA[1])):
                tk = pe.do(lambda e, a=a, b=b, k=k, j=j, t_=t_, ps=ps: e.matmul(
                    ps[:, 512 + t_ * P:640 + t_ * P], b[:, k, t_ * P:(t_ + 1) * P], a[:, k, P:2 * P],
                    start=(k == 0 and j == 0), stop=(k == 7 and j == 2), skip_group_check=True),
                    mark=(k == 7 and j == 2 and t_ == 1))
    W.used[u] = tk
    t_skv = act.do(lambda e, s=s: e.activation(sk[:, :], banks[s][:, 0:T], ACT.Copy), tk)
    t_skv = act.do(lambda e, s=s: e.activation(sv[:, :, :], banks[s][:, 512:768], ACT.Copy), tk)
    free[s] = t_skv

    Sb = [banks[2][:, 0:512], banks[2][:, 512:1024]]
    Tb, Ob = banks[3][:, 0:512], banks[3][:, 512:1024]
    fr = {"S": [None, None], "T": None, "O": None, "L": [None, None], "PT": [None, None], "AB": [None, None],
          "ot": [None, None]}
    n_item = [0]
    y_ready = {}

    def item_local(kind, h):
        i = n_item[0]
        n_item[0] += 1
        b = i % 2
        S, L, mx = Sb[b], Lb[b], sc[:, 64 + 8 * b:72 + 8 * b]
        if kind == "fox":
            row = slice(64 * (h % 2), 64 * (h % 2) + 64)
            qq, kk_, tile = fq[row, h // 2, :], fk[row, h // 2, :], h // 2
            ta = dve.do(lambda e: e.tensor_scalar(cA[b][:, :], cumc[:, :], sel[:, 0:1], sel[:, 8 + h:9 + h],
                                                  ALU.mult, ALU.add), t_c, t_sel, fr["AB"][b])
            tb = dve.do(lambda e: e.tensor_scalar(cB[b][:, :], cumc[:, :], sel[:, 1:2], sel[:, 16 + h:17 + h],
                                                  ALU.mult, ALU.add), t_c, t_sel, fr["AB"][b])
            deps = [t_fq, t_fk]
        else:
            row = slice(64 * (h // 4), 64 * (h // 4) + 64)
            qq, kk_, tile = sq_[row, h % 4, :], sk[row, :], h % 4
            deps = [t_sq, t_skv]
        w = kind == "fox"
        parts = [(0, 0, P), (1, P, 2 * P + P)]
        tk = pe.do(lambda e: e.matmul(S[:, 0:P], qq[:, 0:P], kk_[:, 0:P], start=True, stop=not w,
                                      skip_group_check=True), *deps, fr["S"][b])
        if w:
            tk = pe.do(lambda e: e.matmul(S[:, 0:P], cA[b][:, 0:P], cB[b][:, 0:P], start=False, stop=True,
                                          skip_group_check=True), ta, tb)
        tk = pe.do(lambda e: e.matmul(S[:, P:P + T], qq[:, P:T], kk_[:, 0:T], start=False, stop=not w,
                                      skip_group_check=True))
        if w:
            tk = pe.do(lambda e: e.matmul(S[:, P:P + T], cA[b][:, P:T], cB[b][:, 0:T], start=False, stop=True,
                                          skip_group_check=True))
            fr["AB"][b] = tk
        if w:
            m0, m1 = M3[:, 0:P], M3[:, P:3 * P]
        else:
            m0, m1 = bias[:, h, P:T], bias[:, h, 0:T]
        md = t_m3 if w else t_bias
        dve.do(lambda e: e.tensor_tensor_reduce(L[:, 0:P], S[:, 0:P], m0, 1.0, -3e38, ALU.add, ALU.max, mx[:, 0:1]),
               tk, md, fr["L"][b], mark=False)
        t1 = dve.do(lambda e: e.tensor_tensor_reduce(L[:, P:3 * P], S[:, P:3 * P], m1, 1.0, -3e38, ALU.add, ALU.max,
                                                     mx[:, 1:2]))
        fr["S"][b] = t1
        if w:
            t1 = dve.do(lambda e: e.tensor_scalar(mx[:, 0:2], mx[:, 0:2], -1.0, None, ALU.mult), t1)
        else:
            t1 = dve.do(lambda e: e.tensor_scalar(mx[:, 0:2], mx[:, 0:2], sinkc[:, h:h + 1], -1.0, ALU.max, ALU.mult),
                        t1, t_sink)
            ts = act.do(lambda e: e.activation(mx[:, 4:6], mx[:, 0:2], ACT.Exp, bias=sinkc[:, h:h + 1]), t1)
        act.do(lambda e: e.activation(L[:, 0:P], L[:, 0:P], ACT.Exp, bias=mx[:, 0:1], accum_out=mx[:, 2:3]), t1)
        t2 = act.do(lambda e: e.activation(L[:, P:3 * P], L[:, P:3 * P], ACT.Exp, bias=mx[:, 1:2],
                                           accum_out=mx[:, 3:4]))
        if not w:
            t2 = dve.do(lambda e: e.tensor_tensor(mx[:, 2:4], mx[:, 2:4], mx[:, 4:6], ALU.add), t2, ts)
        t3 = dve.do(lambda e: e.reciprocal(mx[:, 6:8], mx[:, 2:4]), t2)
        dve.do(lambda e: e.tensor_scalar(L[:, 0:P], L[:, 0:P], mx[:, 6:7], None, ALU.mult), t3, mark=False)
        t4 = dve.do(lambda e: e.tensor_scalar(L[:, P:3 * P], L[:, P:3 * P], mx[:, 7:8], None, ALU.mult))
        yield
        for j in range(3):
            tk = pe.do(lambda e, j=j: e.transpose(Tb[:, j * P:(j + 1) * P], L[:, j * P:(j + 1) * P], ident[:, :]),
                       t4, fr["T"], mark=j == 2)
        fr["L"][b] = tk
        t5 = act.do(lambda e: e.activation(PT[b][:, :], Tb[:, 0:384], ACT.Copy), tk, fr["PT"][b])
        fr["T"] = t5
        yield
        val = fv if w else sv
        c = 64 * h if w else 64 * (h // 4)
        first_of_pair = (h % 2 == 0) if w else (h < 4)
        tk = pe.do(lambda e: e.matmul(Ob[row, 0:T], val[:, 0, c:c + 64], PT[b][:, 0:T], start=True, stop=False,
                                      skip_group_check=True), t5, t_fv if w else t_skv, fr["O"])
        tk = pe.do(lambda e: e.matmul(Ob[row, P:T], val[:, 1, c:c + 64], PT[b][:, T:T + P], start=False, stop=True,
                                      skip_group_check=True))
        fr["PT"][b] = tk
        if not first_of_pair:
            o = tile % 2
            fr["O"] = t6 = act.do(lambda e: e.activation(ot[o][:, :], Ob[:, 0:T], ACT.Copy), tk, fr["ot"][o])
            y = (4 if w else 8) + tile
            y_ready[y] = fr["ot"][o] = split(YH[:, y, :], YL[:, y, :], ot[o][:, :], t6, t_mem_done, t_small_done)
        yield

    t_small_done = [t_sel, t_scr]

    def pipeline(items, stages=3):
        live = []
        items = list(items)
        while items or live:
            for g in list(live):
                try:
                    next(g)
                except StopIteration:
                    live.remove(g)
            if items:
                g = item_local(*items.pop(0))
                next(g)
                live.append(g)
            yield

    order = [("fox", h) for h in range(8)] + [("swa", h) for h in (0, 4, 1, 5, 2, 6, 3, 7)]
    bg.append(pipeline(order))

    s, tk = linear(U["cc"], H, 4, r_h)
    t_cc = free[s] = act.do(lambda e, s=s: e.activation(cc[:, :, :], banks[s][:, :], ACT.Copy), tk, tp_h)
    s, tk = linear(U["cu"], H, 4, r_h)
    t_z = free[s] = dve.do(lambda e, s=s: e.tensor_tensor(
        z[:, :, :], banks[s][:, :].rearrange("p (m t) -> p m t", m=4), cc[:, :, :], ALU.mult), tk, t_cc)
    for m in range(4):
        wc = [g_col("conv_w", 4 * i + m) for i in range(3)]
        t1 = dve.do(lambda e, m=m, wc=wc: e.tensor_scalar(cc[:, m, :], z[:, m, :], wc[2], None, ALU.mult), t_z)
        t1 = dve.do(lambda e, m=m, wc=wc: e.scalar_tensor_tensor(
            out=cc[:, m, 1:T], in0=z[:, m, 0:T - 1], scalar=wc[1], in1=cc[:, m, 1:T], op0=ALU.mult, op1=ALU.add), t1)
        t1 = dve.do(lambda e, m=m, wc=wc: e.scalar_tensor_tensor(
            out=cc[:, m, 2:T], in0=z[:, m, 0:T - 2], scalar=wc[0], in1=cc[:, m, 2:T], op0=ALU.mult, op1=ALU.add), t1)
    s, tk = linear(U["cb"], H, 4, r_h)
    t1 = free[s] = dve.do(lambda e, s=s: e.tensor_tensor(
        cc[:, :, :], banks[s][:, :].rearrange("p (m t) -> p m t", m=4), cc[:, :, :], ALU.mult), tk, t1)
    t_conv = split(YH[:, 0:4, :], YL[:, 0:4, :], cc[:, :, :], t1, t_mem_done, t_small_done)
    for i in range(4):
        y_ready[i] = t_conv

    t_gate = []
    for i in range(6):
        s, tk = linear(U["gates"][i], H, 4, r_h)
        free[s] = act.do(lambda e, i=i, s=s: e.activation(gates[:, 4 * i:4 * i + 4, :], banks[s][:, :], ACT.Tanh,
                                                         bias=zero, scale=0.5), tk)
        t_gate.append(free[s])
    t_w_in = tk
    while bg:
        tick()
    t_attn = [fr["ot"][0], fr["ot"][1], fr["L"][0], fr["L"][1], fr["PT"][0], fr["PT"][1]]

    t_x2 = load(x_tm2[:, :, :], d["x"].rearrange("a (t p) n -> p (a t) n", p=P), t_attn)

    def turn_in():
        toks = []
        for g in range(2):
            s = next_set()
            for k in range(4):
                for t_ in range(2):
                    tp = pe.do(lambda e, k=k, t_=t_, g=g, s=s: e.transpose(
                        banks[s][:, k * T + t_ * P:k * T + t_ * P + P],
                        x_tm2[:, t_, (4 * g + k) * P:(4 * g + k + 1) * P], ident[:, :]),
                        t_x2, free[s], mark=(k == 3 and t_ == 1))
            free[s] = act.do(lambda e, g=g, s=s: e.activation(X[:, 4 * g:4 * g + 4, :], banks[s][:, :], ACT.Copy),
                             tp, t_conv)
            toks.append(free[s])
        return toks

    state["sets"] = [0, 1, 2, 3]
    for i in (2, 3):
        free[i] = [fr["S"][0], fr["S"][1], fr["T"], fr["O"]]
    t_mg = [None, None]
    m_ready = {}
    r_y = [{k: y_ready[4 * i + k] for k in range(4)} for i in range(3)]
    for g in range(2):
        m = mg[g]
        for i in range(3):
            s, tk = linear(U["br"][3 * g + i], (YH, YL, 4 * i), 4, r_y[i])
            ps = banks[s][:, :].rearrange("p (m t) -> p m t", m=4)
            gt = gates[:, 8 * i + 4 * g:8 * i + 4 * g + 4, :]
            if i == 0:
                tm = free[s] = dve.do(lambda e, m=m, ps=ps, gt=gt: e.scalar_tensor_tensor(
                    out=m[:, :, :], in0=gt, scalar=1.0, in1=ps, op0=ALU.add, op1=ALU.mult), tk, t_gate, t_attn)
            else:
                tt = free[s] = dve.do(lambda e, ps=ps, gt=gt: e.scalar_tensor_tensor(
                    out=mt[:, :, :], in0=gt, scalar=1.0, in1=ps, op0=ALU.add, op1=ALU.mult), tk, t_attn, tm)
                tm = dve.do(lambda e, m=m: e.tensor_tensor(m[:, :, :], m[:, :, :], mt[:, :, :], ALU.add), tt)
        tok = split(MG[0][:, 4 * g:4 * g + 4, :], MG[1][:, 4 * g:4 * g + 4, :], m[:, :, :], tm, t_attn, scale=0.5)
        for k in range(4):
            m_ready[4 * g + k] = tok
        if g == 0:
            t_xt = turn_in()
    t_br = tk
    t_gates_read = tm

    def add_into(res, units, Hx, ready, t_res):
        toks = []
        for i in range(2):
            s, tk = linear(units[i], Hx, 4, ready)
            ps = banks[s][:, :].rearrange("p (m t) -> p m t", m=4)
            free[s] = dve.do(lambda e, i=i, ps=ps: e.tensor_tensor(
                res[:, 4 * i:4 * i + 4, :], ps, res[:, 4 * i:4 * i + 4, :], ALU.add), tk, t_res)
            toks.append(free[s])
        return toks, tk

    t_X, tk = add_into(X, U["mo"], MG + (0,), m_ready, t_xt)
    t_mo = tk

    def rms(src, toks, *after):
        s = next_set()
        for g in range(2):
            ta = act.do(lambda e, g=g: e.activation(nsq[:, 4 * g:4 * g + 4, :], src[:, 4 * g:4 * g + 4, :],
                                                    ACT.Square), toks[g], *after)
            for k in range(4 * g, 4 * g + 4):
                tk = pe.do(lambda e, k=k, s=s: e.matmul(banks[s][:, 0:T], ones[:, :], nsq[:, k, :],
                                                        start=k == 0, stop=k == 7), ta, t_one, free[s], mark=k == 7)
        t1 = free[s] = act.do(lambda e, s=s: e.activation(nrs[:, :], banks[s][:, 0:T], ACT.Ln, bias=epsc,
                                                          scale=1.0 / 1024), tk, *after)
        return act.do(lambda e: e.activation(nrs[:, :], nrs[:, :], ACT.Exp, bias=zero, scale=-0.5), t1)

    def norm(src, toks, gname, H_, *after):
        t_rs = rms(src, toks, *after)
        ready = {}
        for k in range(8):
            t1 = dve.do(lambda e, k=k: e.scalar_tensor_tensor(out=nh[:, k, :], in0=src[:, k, :],
                                                              scalar=g_col(gname, k), in1=nrs[:, :],
                                                              op0=ALU.mult, op1=ALU.mult), t_rs, toks, *after)
            ready[k] = split(H_[0][:, k, :], H_[1][:, k, :], nh[:, k, :], t1, *after)
        return ready, ready[7]

    r_n, t_n = norm(X, t_X, "xattn_norm_g", HA, t_w_in, t_gates_read)

    for i in range(2):
        s, tk = linear(U["xq"][i], HA + (0,), 4, r_n)
        t_q = free[s] = act.do(lambda e, i=i, s=s: e.activation(
            xq[:, 4 * i:4 * i + 4, :], banks[s][:, :], ACT.Copy, scale=0.0625), tk, t_gates_read, m_ready[7], t_xt)
    t_xq_done = tk
    state["sets"] = [0, 1]
    fr2 = {"S": [free[2], free[2]], "T": free[3], "O": free[3], "L": [None] * 2, "PT": [None] * 2, "xo": [None] * 2}
    o_ready = {}

    def item_cross(h):
        b = h % 2
        S, L, mx = Sb[b], xL[b], sc[:, 64 + 8 * b:72 + 8 * b]
        for t_ in range(2):
            for j in range(2):
                tk = pe.do(lambda e, t_=t_, j=j: e.matmul(
                    S[:, t_ * T:(t_ + 1) * T], xq[:, 2 * h + j, t_ * P:(t_ + 1) * P], xK[:, 2 * h + j, :],
                    start=(j == 0 and t_ == 0), stop=j == 1, skip_group_check=True), t_q, t_xK, fr2["S"][b],
                    mark=(t_ == 1 and j == 1))
        S3 = S.rearrange("p (t n) -> p t n", t=2)
        t1 = dve.do(lambda e: e.reduce_max(mx[:, 0:2], S3, X_AXIS), tk, t_attn)
        t1 = dve.do(lambda e: e.tensor_scalar(mx[:, 0:2], mx[:, 0:2], -1.0, None, ALU.mult), t1)
        for t_ in range(2):
            t2 = act.do(lambda e, t_=t_: e.activation(L[:, t_, :], S[:, t_ * T:(t_ + 1) * T], ACT.Exp,
                                                      bias=mx[:, t_:t_ + 1], accum_out=mx[:, 2 + t_:3 + t_]),
                        t1, fr2["L"][b])
        fr2["S"][b] = t2
        t3 = dve.do(lambda e: e.reciprocal(mx[:, 6:8], mx[:, 2:4]), t2)
        for t_ in range(2):
            t4 = dve.do(lambda e, t_=t_: e.tensor_scalar(L[:, t_, :], L[:, t_, :], mx[:, 6 + t_:7 + t_], None,
                                                         ALU.mult), t3)
        yield
        for kt in range(2):
            for t_ in range(2):
                tk = pe.do(lambda e, kt=kt, t_=t_: e.transpose(
                    Tb[:, kt * T + t_ * P:kt * T + t_ * P + P], L[:, t_, kt * P:(kt + 1) * P], ident[:, :]),
                    t4, fr2["T"], mark=(kt == 1 and t_ == 1))
        fr2["L"][b] = tk
        t5 = fr2["T"] = act.do(lambda e: e.activation(xPT[b][:, :, :], Tb, ACT.Copy), tk, fr2["PT"][b])
        yield
        for dt_ in range(2):
            for kt in range(2):
                tk = pe.do(lambda e, kt=kt, dt_=dt_: e.matmul(
                    Ob[:, dt_ * T:(dt_ + 1) * T], xV[:, kt, h * 256 + dt_ * P:h * 256 + (dt_ + 1) * P],
                    xPT[b][:, kt, :], start=(kt == 0 and dt_ == 0), stop=kt == 1, skip_group_check=True),
                    t5, t_xV, fr2["O"], mark=(kt == 1 and dt_ == 1))
        fr2["PT"][b] = tk
        t6 = fr2["O"] = act.do(lambda e: e.activation(xo[b][:, :, :], Ob, ACT.Copy), tk, fr2["xo"][b])
        tok = fr2["xo"][b] = split(OX[0][:, 2 * h:2 * h + 2, :], OX[1][:, 2 * h:2 * h + 2, :], xo[b][:, :, :], t6, t_br)
        o_ready[2 * h] = o_ready[2 * h + 1] = tok
        yield

    live = []
    for h in list(range(4)) + [None] * 3:
        for g in list(live):
            try:
                next(g)
            except StopIteration:
                live.remove(g)
        if h is not None:
            g = item_cross(h)
            next(g)
            live.append(g)
    state["sets"] = [0, 1, 2, 3]
    free[2] = [fr2["S"][0], fr2["S"][1]]
    free[3] = [fr2["T"], fr2["O"]]
    t_X, t_xo_done = add_into(X, U["xo"], OX + (0,), o_ready, t_X)

    def ffn(units, Hx, ready, *after):
        gu, down = units
        pr = {}
        fs, fp = [None, None], [None, None]
        for i in range(6):
            nm = 4 if i < 5 else 2
            b = i % 2
            s1, tk1 = linear(gu[i][0], Hx, nm, ready)
            t1 = free[s1] = act.do(lambda e, b=b, s1=s1, nm=nm: e.activation(
                silu[b][:, 0:nm * T], banks[s1][:, 0:nm * T], ACT.Silu), tk1, fs[b], *after)
            s2, tk2 = linear(gu[i][1], Hx, nm, ready)
            t2 = free[s2] = dve.do(lambda e, b=b, s2=s2, nm=nm: e.tensor_tensor(
                prod[b][:, 0:nm * T], banks[s2][:, 0:nm * T], silu[b][:, 0:nm * T], ALU.mult), tk2, t1, fp[b], *after)
            fs[b] = t2
            tok = fp[b] = split(PR[0][:, 4 * i:4 * i + nm, :], PR[1][:, 4 * i:4 * i + nm, :], prod[b][:, 0:nm * T],
                                t2, *after)
            for k in range(nm):
                pr[4 * i + k] = tok
        return down, pr, tk2, tok

    r_n, t_n = norm(X, t_X, "ffn_norm_g", HA, t_xq_done, o_ready[7])
    down, pr, tk, t_pr = ffn(U["ffn1"], HA + (0,), r_n, t_xo_done, o_ready[7])
    t_ffn_in = tk
    t_X, t_down = add_into(X, down, PR + (0,), pr, t_X)

    t_rs = rms(X, t_X, t_pr)
    for k in range(8):
        t1 = dve.do(lambda e, k=k: e.scalar_tensor_tensor(out=X[:, k, :], in0=X[:, k, :], scalar=g_col("final_norm_g", k),
                                                          in1=nrs[:, :], op0=ALU.mult, op1=ALU.mult), t_rs)
    t_X = [t1, t1]
    t_X0 = t1
    r_n, t_n = norm(X, t_X, "norm_mix_pre_2", HA, t_ffn_in)
    H = HA + (0,)

    t_ws = load(ws[:, :, :], d["sg_w_2"].rearrange("a g t s -> t (a g) s"), t_down, t_pr)
    bsem = sem("s_bsb")
    sgb = d["sg_b_2"].rearrange("a g t -> (a g) t").rearrange("(m u) t -> u m t", u=2)
    for u in range(2):
        t_bsb = queue.go(bsem, 16 * (u + 1), bsb[64 * u:64 * u + 64, :, :], sgb[u].partition_broadcast(64), t_pr)
    t_lng = load(lng[:, :], d["sg_ln_g_2"].partition_broadcast(P).rearrange("p a n -> p (a n)"), t_pr)
    t_lnb = load(lnb[:, :], d["sg_ln_b_2"].partition_broadcast(P).rearrange("p a n -> p (a n)"), t_pr)
    s = next_set()
    for g in range(8):
        tp = pe.do(lambda e, g=g, s=s: e.transpose(banks[s][:, g * P:(g + 1) * P], ws[:, g, :], ident[:, :]),
                   t_ws, free[s], mark=g == 7)
    t_wsT = free[s] = dve.do(lambda e, s=s: e.tensor_copy(wsT[:, :, :].rearrange("p g t -> p (g t)"), banks[s][:, :]), tp, t_down, t_pr)

    s, tk = linear_tm(U["zv"], H, 512, 0, t_n)
    t1 = free[s] = act.do(lambda e, s=s: e.activation(
        zv[:, :, :], banks[s][:, :].rearrange("p (t n) -> p t n", t=2), ACT.Gelu), tk, t_down)
    st = sc[:, 80:92]
    mv = sc[:, 92:96]
    for t_ in range(2):
        t2 = dve.do(lambda e, t_=t_: e.bn_stats(st[:, 6 * t_:6 * t_ + 6], zv[:, t_, :]), t1)
        t2 = dve.do(lambda e, t_=t_: e.bn_aggr(mv[:, 2 * t_:2 * t_ + 2], st[:, 6 * t_:6 * t_ + 6]), t2)
    var = sc[:, 96:98]
    t2 = dve.do(lambda e: e.tensor_copy(var, mv.rearrange("p (t n) -> p n t", t=2)[:, 1, :]), t2)
    t3 = act.do(lambda e: e.activation(var, var, ACT.Ln, bias=epsc), t2)
    t3 = act.do(lambda e: e.activation(var, var, ACT.Exp, bias=zero, scale=-0.5), t3)
    s, tk = linear(U["zu"], H, 4, r_n)
    t_zu = free[s] = act.do(lambda e, s=s: e.activation(zu[:, :, :], banks[s][:, :], ACT.Gelu), tk, t_down)
    for t_ in range(2):
        t1 = dve.do(lambda e, t_=t_: e.tensor_scalar(zv[:, t_, :], zv[:, t_, :], mv[:, 2 * t_:2 * t_ + 1],
                                                     var[:, t_:t_ + 1], ALU.subtract, ALU.mult), t3)
        t1 = dve.do(lambda e, t_=t_: e.tensor_tensor(zv[:, t_, :], zv[:, t_, :], lng[:, :], ALU.mult), t1, t_lng)
        t1 = dve.do(lambda e, t_=t_: e.tensor_tensor(zv[:, t_, :], zv[:, t_, :], lnb[:, :], ALU.add), t1, t_lnb)
    t_zv = t1
    s = next_set()
    for m in range(4):
        for c in range(2):
            for u in range(2):
                tk = pe.do(lambda e, m=m, c=c, u=u, s=s: e.matmul(
                    banks[s][64 * u:64 * u + 64, m * T + c * P:m * T + c * P + P],
                    zv[:, c, (2 * m + u) * 64:(2 * m + u) * 64 + 64], wsT[:, 2 * m + u, :], start=True, stop=True,
                    skip_group_check=True), t_zv, t_wsT, free[s], mark=(m == 3 and c == 1 and u == 1))
    for c in range(2):
        t1 = dve.do(lambda e, c=c, s=s: e.tensor_tensor(
            bo[:, :, c * P:(c + 1) * P], banks[s][:, :].rearrange("p (m t) -> p m t", m=4)[:, :, c * P:(c + 1) * P],
            bsb[:, :, :], ALU.add), tk, t_bsb, t_n)
    free[s] = t1
    t1 = dve.do(lambda e: e.tensor_tensor(bo[:, :, :], bo[:, :, :], zu[:, :, :], ALU.mult), t1, t_zu)
    t_bo = split(BO[0][:, :, :], BO[1][:, :, :], bo[:, :, :], t1)
    t_sgu = [tk, t1, t_zv]

    lbc = sc[:, 100:116]
    lbm = sc[:, 116:132]
    omb = sc[:, 132:148]
    gam = GC[:, G_AT["lb_gamma_fwd_2"]:G_AT["lb_gamma_fwd_2"] + 16]
    t1 = dve.do(lambda e: e.tensor_tensor(lbm, gam, gam, ALU.subtract), t_gc)
    t1 = act.do(lambda e: e.activation(lbm, lbm, ACT.Exp, bias=zero), t1)
    t1 = dve.do(lambda e: e.reciprocal(lbc, lbm), t1)
    t1 = dve.do(lambda e: e.tensor_tensor(lbm, lbm, lbc, ALU.mult), t1)
    t1 = dve.do(lambda e: e.tensor_tensor(lbc, lbm, lbm, ALU.subtract), t1)
    t_lb = dve.do(lambda e: e.tensor_scalar(omb, lbc, -1.0, 1.0, ALU.mult, ALU.add), t1)

    TINY = float(np.finfo(np.float32).tiny)
    LOW = 2.0 ** -63

    def half_inputs(i, prior):
        uu = U[f"h{i}"]
        got = []
        for j, (name, k_, g_, x_) in enumerate((("ff", kf, Pf, Xf), ("fb", kb, Pb, Xb))):
            s, tk = linear(uu[name], H, 4, r_n)
            act.do(lambda e, s=s, g_=g_: e.activation(g_[:, :, :], banks[s][:, :], ACT.Sigmoid, bias=zero), tk,
                   *prior)
            t1 = free[s] = act.do(lambda e, s=s, k_=k_: e.activation(k_[:, :, :], banks[s][:, :], ACT.Sigmoid,
                                                                     bias=zero, scale=-1.0), tk, *prior)
            for m in range(4):
                c = 8 * j + 4 * i + m
                t2 = dve.do(lambda e, m=m, c=c, k_=k_: e.tensor_scalar(
                    k_[:, m, :], k_[:, m, :], omb[:, c:c + 1], None, ALU.mult), t1, t_lb)
                t3 = dve.do(lambda e, m=m, c=c, g_=g_: e.tensor_scalar(
                    g_[:, m, :], g_[:, m, :], omb[:, c:c + 1], lbc[:, c:c + 1], ALU.mult, ALU.add), t1, t_lb)
            t4 = dve.do(lambda e, g_=g_, x_=x_: e.tensor_scalar(x_[:, :, :], g_[:, :, :], TINY, LOW,
                                                                ALU.max, ALU.min), t3, *prior)
            t5 = dve.do(lambda e, g_=g_: e.tensor_scalar(g_[:, :, :], g_[:, :, :], LOW, None, ALU.max), t3, t4)
            got.append((t2, t4, t5))
        s, tk = linear(uu["q"], H, 4, r_n)
        t1 = act.do(lambda e, s=s: e.activation(q[:, :, :], banks[s][:, :], ACT.Tanh, bias=zero, scale=0.5), tk,
                    *prior)
        t_q_ = dve.do(lambda e, s=s: e.scalar_tensor_tensor(
            out=q[:, :, :], in0=q[:, :, :], scalar=1.0, in1=banks[s][:, :].rearrange("p (m t) -> p m t", m=4),
            op0=ALU.add, op1=ALU.mult), t1)
        free[s] = t_q_
        t_q_ = dve.do(lambda e: e.tensor_scalar(q[:, :, :], q[:, :, :], 0.5, None, ALU.mult), t_q_)
        ready = [t_q_]
        for (t2, t4, t5), g_, x_ in zip(got, (Pf, Pb), (Xf, Xb)):
            act.do(lambda e, g_=g_: e.activation(g_[:, :, :], g_[:, :, :], ACT.Ln, bias=zero), t5, mark=False)
            t6 = act.do(lambda e, x_=x_: e.activation(x_[:, :, :], x_[:, :, :], ACT.Ln, bias=zero,
                                                      scale=2.0 ** 63), t4)
            t7 = dve.do(lambda e, g_=g_, x_=x_: e.tensor_tensor(g_[:, :, :], g_[:, :, :], x_[:, :, :], ALU.add), t6)
            t8 = dve.do(lambda e, x_=x_: e.memset(x_[:, :, :], 0.0), t7)
            ready += [t2, t7, t8]
        return ready

    fr3 = {"S": [None, None], "Q": [None, None], "K": [None, None]}
    a_ready = {}

    def halves(ap, h):
        w = ap.rearrange("p m (b u h) -> p (m b) u h", u=2, h=h)
        return w[:, :, 0, :], w[:, :, 1, :]

    def scores_win(b, w, S, waits):
        for m in range(4):
            tk = pe.do(lambda e, m=m: e.matmul(S[:, m * P:(m + 1) * P], Kt[b][:, m, w * P:(w + 1) * P],
                                               Qt[b][:, m, w * P:(w + 1) * P], start=m == 0, stop=True,
                                               skip_group_check=True), *waits, mark=m == 3)
        return tk

    def mixer(i, ready):
        t_v_ = t_v
        tq = act.do(lambda e: e.activation(Qt[0][:, :, :], q[:, :, :], ACT.Copy), ready, fr3["Q"][0])
        tkk = dve.do(lambda e: e.tensor_tensor(Kt[0][:, :, :], kf[:, :, :], kb[:, :, :], ALU.add), ready, fr3["K"][0])
        t_am = None
        for w in range(2):
            tk = scores_win(0, w, Sb[w], (tq, tkk, fr3["S"][w]))
            t_am = fr3["S"][w] = dve.do(lambda e, w=w: e.tensor_copy(
                Am[:, :, w, w * P:(w + 1) * P], Sb[w].rearrange("p (m t) -> p m t", m=4)), tk, a_free[0])
        fr3["Q"][0] = fr3["K"][0] = tk
        yield
        t_lad = ready
        for n, h in enumerate(LEVELS + [128]):
            b = (n + 1) % 2
            flo, fup = halves(Xf[:, :, :], h)[0], halves(Pf[:, :, :], h)[1]
            blo, bup = halves(Pb[:, :, :], h)[0], halves(Xb[:, :, :], h)[1]
            qlo, qup = halves(Qt[b][:, :, :], h)
            klo, kup = halves(Kt[b][:, :, :], h)
            for o_, i_, f_ in ((qup, fup, fr3["Q"][b]), (qlo, blo, None), (klo, flo, fr3["K"][b]), (kup, bup, None)):
                te = act.do(lambda e, o_=o_, i_=i_: e.activation(o_, i_, ACT.Exp, bias=zero), t_lad, f_)
            tq = dve.do(lambda e, b=b: e.tensor_tensor(Qt[b][:, :, :], Qt[b][:, :, :], q[:, :, :], ALU.mult), te)
            kflo, kbup = halves(kf[:, :, :], h)[0], halves(kb[:, :, :], h)[1]
            dve.do(lambda e, klo=klo, kflo=kflo: e.tensor_tensor(klo, klo, kflo, ALU.mult), te, mark=False)
            tkk = dve.do(lambda e, kup=kup, kbup=kbup: e.tensor_tensor(kup, kup, kbup, ALU.mult), te)
            if h < 128:
                Pfl, Pfu = halves(Pf[:, :, :], h)
                Pbl, Pbu = halves(Pb[:, :, :], h)
                Xfl = halves(Xf[:, :, :], h)[0]
                Xbu = halves(Xb[:, :, :], h)[1]
                shp = [P, 4 * T // (2 * h), h]
                tp1 = pool.do(lambda e, a=Xfl, c=Pfu[:, :, h - 1:h].broadcast_to(shp): e.tensor_tensor(a, a, c, ALU.add), te)
                tp2 = pool.do(lambda e, a=Xbu, c=Pbl[:, :, 0:1].broadcast_to(shp): e.tensor_tensor(a, a, c, ALU.add), te)
                tp3 = dve.do(lambda e, a=Pfu, c=Pfl[:, :, h - 1:h].broadcast_to(shp): e.tensor_tensor(a, a, c, ALU.add), te, tp1)
                tp4 = dve.do(lambda e, a=Pbl, c=Pbu[:, :, 0:1].broadcast_to(shp): e.tensor_tensor(a, a, c, ALU.add), te, tp2)
                t_lad = [tp1, tp2, tp3, tp4]
                for w in range(2):
                    tk = scores_win(b, w, Sb[w], (tq, tkk, fr3["S"][w]))
                    t_am = fr3["S"][w] = dve.do(lambda e, w=w, n=n: e.copy_predicated(
                        Am[:, :, w, w * P:(w + 1) * P], masks[:, n, :].rearrange("p (m t) -> p m t", m=4),
                        Sb[w].rearrange("p (m t) -> p m t", m=4)), tk, t_am, t_ms)
            else:
                for w in range(2):
                    for m in range(4):
                        tk = pe.do(lambda e, m=m, w=w, b=b: e.matmul(
                            Sb[w][:, m * P:(m + 1) * P], Kt[b][:, m, w * P:(w + 1) * P],
                            Qt[b][:, m, (1 - w) * P:(2 - w) * P], start=m == 0, stop=True, skip_group_check=True),
                            tq, tkk, fr3["S"][w], mark=m == 3)
                    t_am = fr3["S"][w] = dve.do(lambda e, w=w: e.tensor_copy(
                        Am[:, :, w, (1 - w) * P:(2 - w) * P], Sb[w].rearrange("p (m t) -> p m t", m=4)), tk, t_am)
            fr3["Q"][b] = fr3["K"][b] = tk
            yield
        for j in range(2):
            B_ = banks[3][:, 512 * j:512 * j + 512]
            for m in (2 * j, 2 * j + 1):
                for w in range(2):
                    tk = pe.do(lambda e, m=m, w=w, B_=B_: e.matmul(
                        B_[:, (m % 2) * T:(m % 2 + 1) * T], v[:, w, (4 * i + m) * P:(4 * i + m + 1) * P], Am[:, m, w, :],
                        start=(m % 2 == 0 and w == 0), stop=w == 1, skip_group_check=True),
                        t_am, t_v_, t_o_free[0], mark=(m % 2 == 1 and w == 1))
            t1 = act.do(lambda e, j=j, B_=B_: e.activation(ho[:, 2 * j:2 * j + 2, :], B_, ACT.Copy), tk)
        a_free[0] = tk
        t_o_free[0] = t1
        t2 = act.do(lambda e: e.activation(hs[:, :, :], ho[:, :, :], ACT.Square), t1)
        yield
        for j in range(2):
            B_ = banks[3][:, 512 * j:512 * j + 512]
            tk = None
            for m in (2 * j, 2 * j + 1):
                tk = pe.do(lambda e, m=m, B_=B_: e.matmul(B_[:, (m % 2) * T:(m % 2 + 1) * T], ones[:, :], hs[:, m, :],
                                                          start=m % 2 == 0, stop=True, skip_group_check=True),
                           t2, t_o_free[0], mark=m % 2 == 1)
            t3 = act.do(lambda e, j=j, B_=B_: e.activation(hr[:, 2 * j:2 * j + 2, :], B_, ACT.Ln, bias=epsc,
                                                           scale=1.0 / 128), tk)
        t_o_free[0] = t3
        t3 = act.do(lambda e: e.activation(hr[:, :, :], hr[:, :, :], ACT.Exp, bias=zero, scale=-0.5), t3)
        for m in range(4):
            t4 = dve.do(lambda e, m=m: e.scalar_tensor_tensor(
                out=ho[:, m, :], in0=ho[:, m, :], scalar=g_col("hg_norm_2", 4 * i + m), in1=hr[:, m, :],
                op0=ALU.mult, op1=ALU.mult), t3)
        t4 = dve.do(lambda e: e.tensor_tensor(ho[:, :, :], ho[:, :, :], zg[:, 4 * i:4 * i + 4, :], ALU.mult), t4, t_zg[0])
        tok = split(AO[0][:, 4 * i:4 * i + 4, :], AO[1][:, 4 * i:4 * i + 4, :], ho[:, :, :], t4, t_bo_done[0], scale=0.5)
        fr3["Q"] = [tok, tok]
        fr3["K"] = [tok, tok]
        for k in range(4):
            a_ready[4 * i + k] = tok
        yield

    a_free, t_o_free, t_zg, t_bo_done = [None], [None], [None], [None]
    ready0 = half_inputs(0, [t_down, t_pr])
    for i in range(2):
        s, tk = linear_tm(U["zi"][i], H, 512, 0, t_n)
        free[s] = act.do(lambda e, i=i, s=s: e.activation(
            v[:, :, 512 * i:512 * i + 512], banks[s][:, :].rearrange("p (t n) -> p t n", t=2), ACT.Copy), tk, t_down)
    t_v = free[s]
    state["sets"] = [0, 1]
    fr3["S"] = [[free[2]], [free[2]]]
    t_o_free[0] = [free[3]]
    fr3["Q"] = [t_sgu + [t_bo], t_sgu + [t_bo]]
    fr3["K"] = [t_sgu + [t_bo], t_sgu + [t_bo]]
    a_free[0] = t_sgu + [t_bo]
    gen0 = mixer(0, ready0)
    bg.append(gen0)
    t_gb = []
    for i in range(2):
        s, tk = linear(U["gb"][i], H, 4, r_n)
        free[s] = act.do(lambda e, i=i, s=s: e.activation(gb[:, 4 * i:4 * i + 4, :], banks[s][:, :], ACT.Tanh,
                                                         bias=zero, scale=0.5), tk, t_n)
        t_gb.append(free[s])
    r_bo = {k: t_bo for k in range(4)}
    for i in range(2):
        s, tk = linear(U["wb2"][i], BO + (0,), 4, r_bo)
        free[s] = t_gb[i] = dve.do(lambda e, i=i, s=s: e.scalar_tensor_tensor(
            out=gb[:, 4 * i:4 * i + 4, :], in0=gb[:, 4 * i:4 * i + 4, :], scalar=1.0,
            in1=banks[s][:, :].rearrange("p (m t) -> p m t", m=4), op0=ALU.add, op1=ALU.mult), tk, t_gb[i])
    t_bo_done[0] = [tk, t_bo]
    for i in range(2):
        s, tk = linear(U["zg"][i], H, 4, r_n)
        zs = zg[:, 4 * i:4 * i + 4, :]
        t1 = act.do(lambda e, zs=zs, s=s: e.activation(zs, banks[s][:, :], ACT.Tanh, bias=zero, scale=0.5), tk, t_n)
        t_zg[0] = free[s] = dve.do(lambda e, zs=zs, s=s: e.scalar_tensor_tensor(
            out=zs, in0=zs, scalar=1.0, in1=banks[s][:, :].rearrange("p (m t) -> p m t", m=4),
            op0=ALU.add, op1=ALU.mult), t1)
    while bg:
        tick()
    ready1 = half_inputs(1, [a_ready[3], a_free[0], t_o_free[0]])
    bg.append(mixer(1, ready1))
    t_ga = []
    for i in range(2):
        s, tk = linear(U["ga"][i], H, 4, r_n)
        free[s] = act.do(lambda e, i=i, s=s: e.activation(ga[:, 4 * i:4 * i + 4, :], banks[s][:, :], ACT.Tanh,
                                                         bias=zero, scale=0.5), tk, t_n)
        t_ga.append(free[s])
    t_in2 = tk
    while bg:
        tick()
    state["sets"] = [0, 1, 2, 3]
    free[2] = [fr3["S"][0], fr3["S"][1]]
    free[3] = t_o_free[0]

    m_ready = {}
    for i in range(2):
        s, tk = linear(U["wa2"][i], AO + (0,), 4, a_ready)
        t1 = free[s] = dve.do(lambda e, i=i, s=s: e.scalar_tensor_tensor(
            out=mtmp[i][:, :, :], in0=ga[:, 4 * i:4 * i + 4, :], scalar=1.0,
            in1=banks[s][:, :].rearrange("p (m t) -> p m t", m=4), op0=ALU.add, op1=ALU.mult), tk, t_ga[i], a_ready[7])
        t1 = dve.do(lambda e, i=i: e.tensor_tensor(mtmp[i][:, :, :], mtmp[i][:, :, :], gb[:, 4 * i:4 * i + 4, :],
                                                   ALU.add), t1, t_gb[i])
        tok = split(ML[0][:, 4 * i:4 * i + 4, :], ML[1][:, 4 * i:4 * i + 4, :], mtmp[i][:, :, :], t1, a_free[0],
                    a_ready[7], scale=0.5)
        for k in range(4):
            m_ready[4 * i + k] = tok
    t_mix = []
    t_wa = tk
    for i in range(2):
        s, tk = linear(U["wo2"][i], ML + (0,), 4, m_ready)
        free[s] = act.do(lambda e, i=i, s=s: e.activation(mix[:, 4 * i:4 * i + 4, :], banks[s][:, :], ACT.Copy), tk,
                         t_wa, m_ready[7])
        t_mix.append(free[s])
    t_wo = tk

    def add_normed(src, toks, gname, t_res, *after):
        t_rs = rms(src, toks, *after)
        out_ = []
        for k in range(8):
            t1 = dve.do(lambda e, k=k: e.scalar_tensor_tensor(out=nh[:, k, :], in0=src[:, k, :],
                                                              scalar=g_col(gname, k), in1=nrs[:, :],
                                                              op0=ALU.mult, op1=ALU.mult), t_rs, *after)
            t1 = dve.do(lambda e, k=k: e.tensor_tensor(X[:, k, :], X[:, k, :], nh[:, k, :], ALU.add), t1, t_res)
            if k in (3, 7):
                out_.append(t1)
        return out_

    t_X = add_normed(mix, t_mix, "norm_mix_post_2", t_X, t_in2, m_ready[7])
    r_n, t_n = norm(X, t_X, "norm_ffn_pre_2", HA, t_X[1])
    down, pr, t_ffn_in, t_pr = ffn(U["ffn2"], HA + (0,), r_n, t_wo, m_ready[7])
    t_ff = []
    for i in range(2):
        s, tk = linear(down[i], PR + (0,), 4, pr)
        free[s] = act.do(lambda e, i=i, s=s: e.activation(mix[:, 4 * i:4 * i + 4, :], banks[s][:, :], ACT.Copy), tk,
                         t_X, t_n)
        t_ff.append(free[s])
    t_down = tk
    t_p = load(p_tm[:, :, :], d["p_2"].rearrange("a b (t p) n -> p (a b t) n", p=P), t_wa, m_ready[7])
    s = next_set()
    for k in range(2):
        for t_ in range(2):
            tp = pe.do(lambda e, k=k, t_=t_, s=s: e.transpose(
                banks[s][:, k * T + t_ * P:k * T + t_ * P + P], p_tm[:, t_, k * P:(k + 1) * P], ident[:, :]),
                t_p, free[s], mark=(k == 1 and t_ == 1))
    t1 = free[s] = act.do(lambda e, s=s: e.activation(pt32[:, :, :], banks[s][:, 0:512], ACT.Copy), tp, t_wa)
    t1 = split(PL[0][:, :, :], PL[1][:, :, :], pt32[:, :, :], t1, t_wa)
    r_p = {0: t1, 1: t1}
    t_pp = []
    for i in range(2):
        s, tk = linear(U["ple"][i], PL + (0,), 4, r_p)
        free[s] = act.do(lambda e, i=i, s=s: e.activation(pp[:, 4 * i:4 * i + 4, :], banks[s][:, :], ACT.Copy, scale=0.5),
                         tk, t_pr)
        t_pp.append(free[s])
    t_X = add_normed(mix, t_ff, "norm_ffn_post_2", t_X, t_pp)
    ready = {}
    for g in range(2):
        tok = split(HA[0][:, 4 * g:4 * g + 4, :], HA[1][:, 4 * g:4 * g + 4, :], X[:, 4 * g:4 * g + 4, :], t_X[g],
                    t_ffn_in)
        for k in range(4):
            ready[4 * g + k] = tok
    t_out = []
    osem = sem("s_out")
    for i in range(2):
        s, tk = linear(U["pg"][i], HA + (0,), 4, ready)
        t1 = free[s] = act.do(lambda e, i=i, s=s: e.activation(tg[i][:, :, :], banks[s][:, :], ACT.Tanh, bias=zero,
                                                               scale=0.5), tk, t_pr)
        t1 = dve.do(lambda e, i=i: e.scalar_tensor_tensor(
            out=tg[i][:, :, :], in0=tg[i][:, :, :], scalar=1.0, in1=pp[:, 4 * i:4 * i + 4, :], op0=ALU.add,
            op1=ALU.mult), t1, t_pp[i])
        t1 = dve.do(lambda e, i=i: e.tensor_tensor(X[:, 4 * i:4 * i + 4, :], X[:, 4 * i:4 * i + 4, :], tg[i][:, :, :],
                                                   ALU.add), t1, tok)
        s = next_set()
        for t_ in range(2):
            for k in range(4):
                tp = pe.do(lambda e, k=k, t_=t_, i=i, s=s: e.transpose(
                    banks[s][:, t_ * 512 + k * P:t_ * 512 + (k + 1) * P], X[:, 4 * i + k, t_ * P:(t_ + 1) * P],
                    ident[:, :]), t1, free[s], mark=(k == 3 and t_ == 1))
        t2 = free[s] = act.do(lambda e, i=i, s=s: e.activation(
            y_tm[:, :, 512 * i:512 * i + 512], banks[s][:, :].rearrange("p (t n) -> p t n", t=2), ACT.Copy), tp, t_down)
        ov = out.rearrange("a (t p) n -> p (a t) n", p=P)
        queue.go(osem, 16 * (i + 1), ov[:, :, 512 * i:512 * i + 512], y_tm[:, :, 512 * i:512 * i + 512], t2)

    sp.items.append(("wait", osem, 32))
    assert W.done == len(W.units)

    with nc.Block() as block:
        @block.sync
        def _(e):
            sp.replay(e)

        @block.tensor
        def _(e):
            pe.replay(e)

        @block.scalar
        def _(e):
            act.replay(e)

        @block.vector
        def _(e):
            dve.replay(e)

        @block.gpsimd
        def _(e):
            pool.replay(e)


_INS = ["x", "mem", "mix_norm_g", "w_in", "forget_bias", "conv_w", "sink", "w_branch", "w_mix_out", "rel_bias",
        "xattn_norm_g", "mem_norm_g", "w_xq", "w_xkv", "w_xo", "ffn_norm_g", "w_ffn_gate", "w_ffn_up", "w_ffn_down",
        "final_norm_g", "p_2", "norm_mix_pre_2", "w_in_2", "lb_gamma_fwd_2", "lb_gamma_bwd_2", "hg_norm_2",
        "sg_w_2", "sg_b_2", "sg_ln_g_2", "sg_ln_b_2", "w_a_2", "w_b_2", "w_out_2", "norm_mix_post_2",
        "norm_ffn_pre_2", "w_gate_2", "w_up_2", "w_down_2", "norm_ffn_post_2", "w_ple_2", "w_ple_gate_2"]


def kernel(**inputs):
    import concourse.bacc as _bacc
    from concourse.bass_utils import run_bass_kernel_spmd as _run

    nc = _bacc.Bacc("TRN2", target_bir_lowering=False, num_devices=1)
    arrays, d = {}, {}
    for name in _INS:
        a = np.ascontiguousarray(inputs[name])
        arrays[f"in_{name}"] = a
        d[name] = nc.dram_tensor(f"in_{name}", a.shape, mybir.dt.from_np(a.dtype), kind="ExternalInput").ap()
    for name, a in constants().items():
        arrays[name] = a
        d[name] = nc.dram_tensor(name, a.shape, mybir.dt.from_np(a.dtype), kind="ExternalInput").ap()
    out = nc.dram_tensor("out_0", (1, 256, 1024), F32, kind="ExternalOutput").ap()
    build(nc, d, out)
    r = _run(nc, [arrays], core_ids=[0])
    return r.results[0]["out_0"]
```
